# Optimizing a Trainium2 kernel written in Bass

```python
import math, functools
import jax, jax.numpy as jnp
from jax import lax
import numpy as np

D_MODEL = 1024
BATCH = 1
SEQ = 512
DEPTH = 2
DEC_BATCH = 8
DEC_SEQ = 16
PAST_LEN = 256

CHUNK = 64
Q_BLOCK = 128
N_EVEN = (DEPTH + 1) // 2
N_ODD = DEPTH // 2
ALPHA = (2 * DEPTH) ** 0.25
BETA = (8 * DEPTH) ** -0.25
EPS = 1e-5
NEG_INF = -1e30
MLA_HEADS = 8
Q_LORA = 256
KV_LORA = 128
MLA_NOPE_DIM = 64
MLA_ROPE_DIM = 32
MLA_QK_DIM = MLA_NOPE_DIM + MLA_ROPE_DIM
MLA_V_DIM = 64
MLA_ROPE_THETA = 10000.0
MLA_W = MLA_HEADS * MLA_V_DIM
DIFF_HEADS = 4
DIFF_HD = 64
DIFF_ROT = DIFF_HD // 4
ROPE_THETA = 500000.0
DIFF_W = DIFF_HEADS * 2 * DIFF_HD
SB_HEADS = 16
SB_HD = 64
SB_W = SB_HEADS * SB_HD
EVEN_SECTIONS = (Q_LORA, KV_LORA, MLA_ROPE_DIM, MLA_W, DIFF_W, DIFF_W, DIFF_W, DIFF_W)
EVEN_IN = Q_LORA + KV_LORA + MLA_ROPE_DIM + MLA_W + 4 * DIFF_W
EVEN_OUT = MLA_W + DIFF_W
DV_START = Q_LORA + KV_LORA + MLA_ROPE_DIM + MLA_W + 2 * DIFF_W

kernel_name = 'hybrid_stream_mla_diff_stickbreak_step'

def _layernorm(x, g, b):
    xf = x.astype(jnp.float32)
    mu = jnp.mean(xf, axis=-1, keepdims=True)
    xc = xf - mu
    var = jnp.mean(xc * xc, axis=-1, keepdims=True)
    return (xc * lax.rsqrt(var + EPS) * g.astype(jnp.float32) + b.astype(jnp.float32)).astype(x.dtype)

def _rmsnorm(x, g):
    xf = x.astype(jnp.float32)
    ms = jnp.mean(xf * xf, axis=-1, keepdims=True)
    return (xf * lax.rsqrt(ms + EPS) * g.astype(jnp.float32)).astype(x.dtype)

def _rope(x, pos, rot_dim, theta):
    half = rot_dim // 2
    inv = jnp.exp(-math.log(theta) * jnp.arange(half, dtype=jnp.float32) * (2.0 / rot_dim))
    ang = pos.astype(jnp.float32)[:, None] * inv[None, :]
    shape = (pos.shape[0],) + (1,) * (x.ndim - 3) + (half,)
    cos = jnp.cos(ang).reshape(shape).astype(x.dtype)
    sin = jnp.sin(ang).reshape(shape).astype(x.dtype)
    x1, x2, rest = x[..., :half], x[..., half:rot_dim], x[..., rot_dim:]
    return jnp.concatenate([x1 * cos - x2 * sin, x1 * sin + x2 * cos, rest], axis=-1)

def _split_cols(h, sizes):
    offs = np.cumsum(np.array(sizes))[:-1].tolist()
    return jnp.split(h, offs, axis=-1)

def _chunk_mask(qpos, kpos):
    return (kpos[None, :] // CHUNK) <= (qpos[:, None] // CHUNK)

def _mla_core(q_abs, q_rope, ckv, krope, qpos, kpos):
    s = (jnp.einsum('bqhc,bkc->bhqk', q_abs, ckv) + jnp.einsum('bqhr,bkr->bhqk', q_rope, krope)).astype(jnp.float32)
    s = jnp.where(_chunk_mask(qpos, kpos), s * (MLA_QK_DIM ** -0.5), NEG_INF)
    p = jax.nn.softmax(s, axis=-1).astype(ckv.dtype)
    return jnp.einsum('bhqk,bkc->bqhc', p, ckv)

def _diff_core(q, k, v, qpos, kpos, lam):
    s = jnp.einsum('bqhid,bkhid->bhiqk', q, k).astype(jnp.float32) * (DIFF_HD ** -0.5)
    s = jnp.where(_chunk_mask(qpos, kpos), s, NEG_INF)
    p = jax.nn.softmax(s, axis=-1)
    a = (p[:, :, 0] - lam * p[:, :, 1]).astype(v.dtype)
    return jnp.einsum('bhqk,bkhe->bqhe', a, v)

def _sb_core(q, k, v, qpos, kpos):
    z = jnp.einsum('bqhd,bkhd->bhqk', q, k).astype(jnp.float32) * (SB_HD ** -0.5)
    valid = kpos[None, :] < qpos[:, None]
    log_beta = jax.nn.log_sigmoid(z)
    log_rem = jnp.where(valid, jax.nn.log_sigmoid(-z), 0.0)
    later = lax.cumsum(log_rem, axis=3, reverse=True) - log_rem
    a = jnp.where(valid, jnp.exp(log_beta + later), 0.0).astype(v.dtype)
    return jnp.einsum('bhqk,bkhd->bqhd', a, v)

def _sweep_queries(core, q_args, kv_args, seq_len):
    nb = seq_len // Q_BLOCK
    kpos = jnp.arange(seq_len, dtype=jnp.int32)

    def to_blocks(a):
        return jnp.swapaxes(a.reshape((a.shape[0], nb, Q_BLOCK) + a.shape[2:]), 0, 1)

    def one_block(args):
        i, qb = args
        qpos = i * Q_BLOCK + jnp.arange(Q_BLOCK, dtype=jnp.int32)
        return core(*qb, *kv_args, qpos, kpos)

    out = lax.map(one_block, (jnp.arange(nb, dtype=jnp.int32), tuple(to_blocks(a) for a in q_args)))
    out = jnp.swapaxes(out, 0, 1)
    return out.reshape((out.shape[0], seq_len) + out.shape[3:])

def _even_layer(x, pos, caches, prm, lam_init):
    (w_in, q_g, w_uq, kv_g, w_uk, w_uv, lam_q, lam_k, subln_g, w_out, ln_g, ln_b) = prm
    b, s, _ = x.shape
    h = x @ w_in
    q_lat, ckv, krope, g_mla, dq, dk, dv, g_diff = _split_cols(h, EVEN_SECTIONS)
    q = (_rmsnorm(q_lat, q_g) @ w_uq).reshape(b, s, MLA_HEADS, MLA_QK_DIM)
    q_rope = _rope(q[..., MLA_NOPE_DIM:], pos, MLA_ROPE_DIM, MLA_ROPE_THETA)
    q_abs = jnp.einsum('bshn,chn->bshc', q[..., :MLA_NOPE_DIM], w_uk)
    ckv = _rmsnorm(ckv, kv_g)
    krope = _rope(krope, pos, MLA_ROPE_DIM, MLA_ROPE_THETA)
    dq = _rope(dq.reshape(b, s, DIFF_HEADS, 2, DIFF_HD), pos, DIFF_ROT, ROPE_THETA)
    dk = _rope(dk.reshape(b, s, DIFF_HEADS, 2, DIFF_HD), pos, DIFF_ROT, ROPE_THETA)
    dv = dv.reshape(b, s, DIFF_HEADS, 2 * DIFF_HD)
    lq = lam_q.astype(jnp.float32)
    lk = lam_k.astype(jnp.float32)
    lam = jnp.exp(jnp.sum(lq[0] * lk[0])) - jnp.exp(jnp.sum(lq[1] * lk[1])) + lam_init
    diff_core = functools.partial(_diff_core, lam=lam)
    if caches is None:
        o_lat = _sweep_queries(_mla_core, (q_abs, q_rope), (ckv, krope), s)
        o_diff = _sweep_queries(diff_core, (dq,), (dk, dv), s)
    else:
        ckv_c, krope_c, dk_c, dv_c = caches
        kpos = jnp.arange(ckv_c.shape[1] + s, dtype=jnp.int32)
        o_lat = _mla_core(q_abs, q_rope, jnp.concatenate([ckv_c, ckv], axis=1),
                          jnp.concatenate([krope_c, krope], axis=1), pos, kpos)
        o_diff = diff_core(dq, jnp.concatenate([dk_c, dk], axis=1), jnp.concatenate([dv_c, dv], axis=1), pos, kpos)
    o_mla = jnp.einsum('bshc,chv->bshv', o_lat, w_uv).reshape(b, s, MLA_W)
    o_diff = (_rmsnorm(o_diff, subln_g) * (1.0 - lam_init)).reshape(b, s, DIFF_W)
    o = jnp.concatenate([o_mla * jax.nn.silu(g_mla), o_diff * jax.nn.silu(g_diff)], axis=-1) @ w_out
    y = _layernorm(ALPHA * x + o, ln_g, ln_b)
    return y, (ckv, krope, dk, dv)

def _odd_layer(x, pos, caches, prm):
    w_in, w_out, ln_g, ln_b = prm
    b, s, _ = x.shape
    q, k, v, g = _split_cols(x @ w_in, (SB_W, SB_W, SB_W, SB_W))
    q = q.reshape(b, s, SB_HEADS, SB_HD)
    k = k.reshape(b, s, SB_HEADS, SB_HD)
    v = v.reshape(b, s, SB_HEADS, SB_HD)
    if caches is None:
        o = _sweep_queries(_sb_core, (q,), (k, v), s)
    else:
        k_c, v_c = caches
        kpos = jnp.arange(k_c.shape[1] + s, dtype=jnp.int32)
        o = _sb_core(q, jnp.concatenate([k_c, k], axis=1), jnp.concatenate([v_c, v], axis=1), pos, kpos)
    o = (o.reshape(b, s, SB_W) * jax.nn.silu(g)) @ w_out
    y = _layernorm(ALPHA * x + o, ln_g, ln_b)
    return y, (k, v)

def setup_inputs(seed: int = 0) -> dict:
    key = jax.random.key(seed)
    ks = jax.random.split(key, 24)

    def nrm(k, shape, scale):
        return jax.random.normal(k, shape, jnp.float32) * scale

    w_in_even = nrm(ks[8], (N_EVEN, D_MODEL, EVEN_IN), D_MODEL ** -0.5)
    w_in_even = w_in_even.at[:, :, DV_START:DV_START + DIFF_W].multiply(BETA)
    w_in_odd = nrm(ks[19], (N_ODD, D_MODEL, 4 * SB_W), D_MODEL ** -0.5)
    w_in_odd = w_in_odd.at[:, :, 2 * SB_W:3 * SB_W].multiply(BETA)
    return {
        'x_prompt': nrm(ks[0], (BATCH, SEQ, D_MODEL), 1.0),
        'x_sample': nrm(ks[1], (DEC_BATCH, DEC_SEQ, D_MODEL), 1.0),
        'cache_mla_ckv': nrm(ks[2], (N_EVEN, DEC_BATCH, PAST_LEN, KV_LORA), 1.0),
        'cache_mla_krope': nrm(ks[3], (N_EVEN, DEC_BATCH, PAST_LEN, MLA_ROPE_DIM), 1.0),
        'cache_diff_k': nrm(ks[4], (N_EVEN, DEC_BATCH, PAST_LEN, DIFF_HEADS, 2, DIFF_HD), 1.0),
        'cache_diff_v': nrm(ks[5], (N_EVEN, DEC_BATCH, PAST_LEN, DIFF_HEADS, 2 * DIFF_HD), BETA),
        'cache_sb_k': nrm(ks[6], (N_ODD, DEC_BATCH, PAST_LEN, SB_HEADS, SB_HD), 1.0),
        'cache_sb_v': nrm(ks[7], (N_ODD, DEC_BATCH, PAST_LEN, SB_HEADS, SB_HD), BETA),
        'w_in_even': w_in_even,
        'q_norm_g': 1.0 + nrm(ks[9], (N_EVEN, Q_LORA), 0.02),
        'w_uq': nrm(ks[10], (N_EVEN, Q_LORA, MLA_HEADS * MLA_QK_DIM), Q_LORA ** -0.5),
        'kv_norm_g': 1.0 + nrm(ks[11], (N_EVEN, KV_LORA), 0.02),
        'w_uk': nrm(ks[12], (N_EVEN, KV_LORA, MLA_HEADS, MLA_NOPE_DIM), KV_LORA ** -0.5),
        'w_uv': nrm(ks[13], (N_EVEN, KV_LORA, MLA_HEADS, MLA_V_DIM), KV_LORA ** -0.5 * BETA),
        'diff_lambda_q': nrm(ks[14], (N_EVEN, 2, DIFF_HD), 0.1),
        'diff_lambda_k': nrm(ks[15], (N_EVEN, 2, DIFF_HD), 0.1),
        'diff_subln_g': 1.0 + nrm(ks[16], (N_EVEN, 2 * DIFF_HD), 0.02),
        'w_out_even': nrm(ks[17], (N_EVEN, EVEN_OUT, D_MODEL), EVEN_OUT ** -0.5 * BETA),
        'ln_even_g': 1.0 + nrm(ks[18], (N_EVEN, D_MODEL), 0.02),
        'ln_even_b': nrm(ks[20], (N_EVEN, D_MODEL), 0.02),
        'w_in_odd': w_in_odd,
        'w_out_odd': nrm(ks[21], (N_ODD, SB_W, D_MODEL), SB_W ** -0.5 * BETA),
        'ln_odd_g': 1.0 + nrm(ks[22], (N_ODD, D_MODEL), 0.02),
        'ln_odd_b': nrm(ks[23], (N_ODD, D_MODEL), 0.02),
    }

def reference(x_prompt, x_sample, cache_mla_ckv, cache_mla_krope, cache_diff_k, cache_diff_v, cache_sb_k, cache_sb_v,
              w_in_even, q_norm_g, w_uq, kv_norm_g, w_uk, w_uv, diff_lambda_q, diff_lambda_k, diff_subln_g,
              w_out_even, ln_even_g, ln_even_b, w_in_odd, w_out_odd, ln_odd_g, ln_odd_b):
    pos_p = jnp.arange(x_prompt.shape[1], dtype=jnp.int32)
    pos_s = cache_sb_k.shape[2] + jnp.arange(x_sample.shape[1], dtype=jnp.int32)
    yp, ys = x_prompt, x_sample
    even_p, even_s, odd_p, odd_s = [], [], [], []
    for layer in range(DEPTH):
        i = layer // 2
        if layer % 2 == 0:
            prm = (w_in_even[i], q_norm_g[i], w_uq[i], kv_norm_g[i], w_uk[i], w_uv[i], diff_lambda_q[i],
                   diff_lambda_k[i], diff_subln_g[i], w_out_even[i], ln_even_g[i], ln_even_b[i])
            lam_init = 0.8 - 0.6 * math.exp(-0.3 * layer)
            yp, st_p = _even_layer(yp, pos_p, None, prm, lam_init)
            ys, st_s = _even_layer(ys, pos_s, (cache_mla_ckv[i], cache_mla_krope[i], cache_diff_k[i], cache_diff_v[i]),
                                   prm, lam_init)
            even_p.append(st_p)
            even_s.append(st_s)
        else:
            prm = (w_in_odd[i], w_out_odd[i], ln_odd_g[i], ln_odd_b[i])
            yp, st_p = _odd_layer(yp, pos_p, None, prm)
            ys, st_s = _odd_layer(ys, pos_s, (cache_sb_k[i], cache_sb_v[i]), prm)
            odd_p.append(st_p)
            odd_s.append(st_s)
    return (yp, ys,
            jnp.stack([t[0] for t in even_p]), jnp.stack([t[1] for t in even_p]),
            jnp.stack([t[2] for t in even_p]), jnp.stack([t[3] for t in even_p]),
            jnp.stack([t[0] for t in odd_p]), jnp.stack([t[1] for t in odd_p]),
            jnp.stack([t[0] for t in even_s]), jnp.stack([t[1] for t in even_s]),
            jnp.stack([t[2] for t in even_s]), jnp.stack([t[3] for t in even_s]),
            jnp.stack([t[0] for t in odd_s]), jnp.stack([t[1] for t in odd_s]))


_drawn_inputs = setup_inputs


def setup_inputs(seed=0):
    import zlib

    import numpy as np

    out = dict(_drawn_inputs(seed))
    spreads = {}
    factors = {'cache_mla_ckv': 7.857,
     'cache_mla_krope': 8.0,
     'cache_sb_k': 6.504,
     'cache_sb_v': 2.804,
     'q_norm_g': 8.0,
     'w_uq': 6.486,
     'w_uk': 7.055,
     'w_uv': 5.481,
     'diff_lambda_k': 3.267,
     'diff_subln_g': 27.884,
     'ln_even_g': 2.887,
     'ln_even_b': 2.932,
     'ln_odd_g': 7.945,
     'ln_odd_b': 8.206}
    for name, (base, spread) in spreads.items():
        noise = np.random.default_rng([zlib.crc32(name.encode()), seed]).standard_normal(out[name].shape)
        drawn = base * np.exp(spread * noise) if base else spread * noise
        out[name] = __import__('jax').numpy.asarray(drawn.astype(out[name].dtype))
    for name, factor in factors.items():
        out[name] = (out[name] * factor).astype(out[name].dtype)
    return out
```

```python
from contextlib import ExitStack
import math

import numpy as np

import concourse.bass as bass
from concourse import mybir

F32 = mybir.dt.float32
BF16 = mybir.dt.bfloat16
ALU = mybir.AluOpType
ACT = mybir.ActivationFunctionType
AX_X = mybir.AxisListType.X

P = 128
D = 1024
KD = D // P
SEQ, STREAMS, NEW, PAST = 512, 8, 16, 256
PT_TILES = SEQ // P
TILES = PT_TILES + 1
S_TILE = PT_TILES
TOK = TILES * P
KEYS = PAST + NEW
CKV_SLOTS = 5
MASKS = 2 * P + NEW
SMALL = 13
ALPHA = 4 ** 0.25
EPS = 1e-5
MH, NOPE, ROT, MV = 8, 64, 32, 64
QK = NOPE + ROT
QL, KVL = 256, 128
SEC_A = QL + KVL + ROT
DH, HD, DROT = 4, 64, 16
MLA_W = MH * MV
DIFF_W = DH * 2 * HD
LAM_INIT = 0.8 - 0.6 * math.exp(-0.3 * 0)
MLA_SCALE = QK ** -0.5
HEAD_SCALE = HD ** -0.5
GROUPS, GH = 4, 4
GW = GH * HD
DIFF_ROWS = DH * NEW



def pipeline(steps, fillers, after=None, ahead=None):
    jobs, done, later = [], 0, {}
    turns = len(steps) + 3
    for job in (ahead(steps[0]) if ahead else []):
        jobs.append(job)
    for i in range(turns):
        if i < len(steps):
            jobs.append(("score", steps[i]))
            if steps[i][0] == "D":
                jobs.append(("score2", steps[i]))
            if ahead and i + 1 < len(steps):
                jobs += ahead(steps[i + 1])
        if 1 <= i <= len(steps):
            jobs.append(("weigh", steps[i - 1]))
        want = len(fillers) * (i + 1) // turns
        jobs += fillers[done:want]
        done = want
        jobs += later.pop(i, [])
        if 2 <= i < len(steps) + 2:
            jobs.append(("turn", steps[i - 2]))
        if 3 <= i:
            jobs.append(("value", steps[i - 3]))
            for turns_on, job in (after(steps[i - 3]) if after else []):
                later.setdefault(i + turns_on, []).append(job)
    for i in sorted(later):
        jobs += later[i]
    return jobs


def mingle(prompt, samples):
    n = len(prompt) // len(samples)
    return [s for i, one in enumerate(samples) for s in prompt[i * n:(i + 1) * n] + [one]]


def make_schedule():
    tiles = range(TILES)
    jobs = [("xT", 0, t, h) for t in tiles for h in range(2)]
    jobs += [("A", t) for t in tiles] + [("rms",)]
    jobs += [("G", t) for t in tiles]
    jobs += [("latT", t) for t in tiles]
    for t in tiles:
        jobs += [("uq", t, 0), ("uq", t, 1), ("uqrope", t)]
        if t:
            jobs += [("qT", t - 1, 0), ("qT", t - 1, 1)]
    jobs += [("kn", h) for h in range(MH)]
    jobs += [("qT", S_TILE, 0), ("qT", S_TILE, 1)]
    jobs += [("vm", t) for t in range(PT_TILES)] + [("wukT", 0), ("wukT", 1)] + [("qa", 0), ("qa", 1)]

    fill = later_projections(tiles)
    steps = mingle([("M", t, h) for t in range(PT_TILES) for h in range(MH)], [("MS", b) for b in range(STREAMS)])
    jobs += pipeline(steps, fill, ahead=lambda s: [("cacheT",) + s] if s[0] == "MS" else [])
    jobs += [("om",), ("qblocks",)]

    fill = [("ogT", t, 0) for t in range(2)]
    for t in tiles:
        fill += [("outp", 0, t, 0), ("outp", 0, t, 1)] + ([("ogT", t + 2, 0)] if t + 2 < TILES else [])
    steps = mingle([("D", t, h) for t in range(PT_TILES) for h in range(DH)], [("DS", b) for b in range(STREAMS)])
    jobs += pipeline(
        steps, fill,
        ahead=lambda s: [("cacheT",) + s + (k,) for k in range(2)] if s[0] == "DS" else [],
        after=lambda s: [(1, ("post", s[1])), (3, ("ogT", s[1], 1))] if s[0] == "D" and s[2] == DH - 1 else [])
    jobs += [("od",), ("post", S_TILE)]
    for t in tiles:
        jobs += [("out", 0, t, 0), ("out", 0, t, 1), ("ln", 0, t)]
        if t == 0:
            jobs += [("ogT", S_TILE, 1)]
        else:
            jobs += [("xT", 1, t - 1, 0), ("xT", 1, t - 1, 1)]
    jobs += [("xT", 1, S_TILE, 0), ("xT", 1, S_TILE, 1)]

    def project(g):
        js = [("kv", g, 0)]
        for t in tiles[1:]:
            js += [("kv", g, t), ("kT", g, t - 1)]
        js += [("q", g, 0), ("kT", g, S_TILE), ("q", g, 1), ("qs", g), ("gblocks", g)]
        return js + [("g", g, t) for t in range(PT_TILES)] + [("gs", g)]

    jobs += project(0)
    for g in range(GROUPS):
        steps = mingle([("B", g, t, h) for t in range(PT_TILES) for h in range(GH)],
                       [("BS", g, p) for p in range(STREAMS // 2)])
        fill = project(g + 1) if g + 1 < GROUPS else [("outp", 1, t, h) for t in tiles for h in range(2)]
        jobs += pipeline(
            steps, fill,
            ahead=lambda s: [("cacheT",) + s + (k,) for k in range(2)] if s[0] == "BS" else [],
            after=lambda s: [(1, ("oT", s[1], s[2]))] if s[0] == "B" and s[3] == GH - 1 else [])
    for t in tiles:
        jobs += [("out", 1, t, 0), ("out", 1, t, 1), ("ln", 1, t)]
    return jobs


def later_projections(tiles):
    names = [("dq", t) for t in tiles] + [("dk", t) for t in tiles]
    fill = []
    for n, job in enumerate(names):
        fill.append(job)
        if n:
            kind, t = names[n - 1]
            fill.append((kind + "T", t))
    fill += [("dv", 0), ("dkT", S_TILE)]
    return fill + [("dv", t) for t in tiles[1:]] + [("gd", t) for t in tiles]


BANKS = {"proj": 2, "score": 2, "turn": 3, "value": 1}
RING_OF = {}
for _k in ("A", "G", "uq", "kn", "vm", "qa", "dq", "dk", "dv", "gd", "om", "out", "outp", "kv", "q", "qs", "g", "gs"):
    RING_OF[_k] = "proj"
for _k in ("xT", "latT", "qT", "wukT", "dqT", "dkT", "cacheT", "turn", "ogT", "od", "kT", "oT"):
    RING_OF[_k] = "turn"
for _k in ("score", "score2"):
    RING_OF[_k] = "score"
RING_OF["value"] = "value"


def assign_banks(schedule):
    uses = {r: 0 for r in BANKS}
    where = {}
    for job in schedule:
        ring = RING_OF.get(job[0])
        if ring:
            n = uses[ring]
            where[job] = (f"{ring}{n % BANKS[ring]}", n // BANKS[ring] + 1)
            uses[ring] = n + 1
    return where


def turn_blocks(step):
    if step[0] in ("M", "D"):
        return [(j * P, P) for j in range(step[1] + 1)]
    if step[0] == "B":
        return [(j * P, P) for j in range(step[2] + 1)]
    return [(0, P), (P, P), (PAST, NEW)]


def width(step):
    a, n = turn_blocks(step)[-1]
    return a + n




def trunk_kernel(nc, a, out):
    schedule = make_schedule()
    where = assign_banks(schedule)
    steps = [j[1] for j in schedule if j[0] == "score"]
    nth = {s: i for i, s in enumerate(steps)}
    exp_steps = [s for s in steps if s[0] in ("M", "MS", "D", "DS")]
    sb_steps = [s for s in steps if s[0] in ("B", "BS")]

    ctx = ExitStack()

    def sem(name):
        return ctx.enter_context(nc.semaphore(name))

    def alloc(stack, name, shape, dt=F32):
        return stack.enter_context(nc.sbuf_tensor(name, [P] + shape, dt))

    with ctx:
        def sb(name, shape, dt=F32):
            return alloc(ctx, name, shape, dt)

        x_sb = sb("x_sb", [TILES, D])
        xT = sb("xT", [KD, TOK])
        w_sb = sb("w_sb", [2, KD, 512])
        probs = sb("probs", [3, 512])
        work8 = sb("work8", [4, 512])
        probs2 = work8[:, 0:2, :]
        wT = work8[:, 2:4, :]
        latT = work8[:, :, :].rearrange("p a b -> p (a b)")[:, 0:3 * TOK].rearrange("p (a b) -> p a b", a=3)
        ident = sb("ident", [P])
        identb = sb("identb", [P], BF16)
        mask_chunk = sb("mask_chunk", [P], BF16)
        mask_causal = sb("mask_causal", [P], BF16)
        mask_new = sb("mask_new", [NEW], BF16)
        stats = sb("stats", [2, 8])
        stats2 = sb("stats2", [2, 8])
        coef = sb("coef", [2, 8])
        bn = sb("bn", [2, 6])
        mv = sb("mv", [2])
        rstd = sb("rstd", [1])
        minus_half = sb("minus_half", [10])

        l0 = ExitStack()
        lat = alloc(l0, "lat", [TILES, SEC_A])
        gates = alloc(l0, "gates", [TILES, D])
        dv = alloc(l0, "dv", [TILES, DIFF_W])
        diffT = alloc(l0, "diffT", [2, DH, TOK])
        mlaK = alloc(l0, "mlaK", [MH, SEQ])
        vm = alloc(l0, "vm", [PT_TILES, MLA_W])
        uq = alloc(l0, "uq", [2, MH * QK])
        ckvTs = alloc(l0, "ckvTs", [P])
        qr = alloc(l0, "qr", [STREAMS, P])
        krTs = alloc(l0, "krTs", [P])
        ckv_c = alloc(l0, "ckv_c", [CKV_SLOTS, 2, KVL])
        kr_c = alloc(l0, "kr_c", [(2 + 2 * STREAMS) * ROT])
        w_uq = alloc(l0, "w_uq", [2, MH * QK])
        w_uk = alloc(l0, "w_uk", [MH * NOPE])
        w_uv = alloc(l0, "w_uv", [MLA_W])
        g_q = alloc(l0, "g_q", [QL])
        g_kv = alloc(l0, "g_kv", [KVL])
        g_sub = alloc(l0, "g_sub", [2 * HD])
        lam = alloc(l0, "lam", [8])
        ropem = alloc(l0, "ropem", [TILES, ROT])
        roped = alloc(l0, "roped", [TILES, DROT])
        rtmp = alloc(l0, "rtmp", [2, P])
        newv = alloc(l0, "newv", [2, 512])
        sel = alloc(l0, "sel", [DIFF_ROWS])
        sign = alloc(l0, "sign", [2])
        csel = alloc(l0, "csel", [2, DIFF_ROWS])
        ss = alloc(l0, "ss", [3, 10])
        qT = x_sb[:, :, :].rearrange("p a b -> p (a b)").rearrange("p (h n) -> p h n", h=MH)
        flat = lambda b: b[:, :, :].rearrange("p a b -> p (a b)")
        lam4 = flat(rtmp).rearrange("p (a b) -> p a b", a=4)
        rot = flat(uq)[:, 0:1024].rearrange("p (a b) -> p a b", a=2)
        sq2 = flat(uq)[:, 1024:1536]
        qa = flat(work8)[:, 0:1024].rearrange("p (b n) -> p b n", b=STREAMS)
        wukT = flat(probs)[:, 512:1536].rearrange("p (h n) -> p h n", h=MH)
        o_mlaT = flat(lat)[:, 0:1024].rearrange("p (h n) -> p h n", h=MH)
        ckv_cT = flat(lat)[:, 1024:1536].rearrange("p (a b) -> p a b", a=2)
        kr_cT = flat(lat)[:, 1536:2048].rearrange("p (a b) -> p a b", a=2)
        newckv = flat(newv).rearrange("p (b c) -> p b c", b=STREAMS)
        qblk = flat(w_uq)[:, 0:1024].rearrange("p (b h n) -> p b h n", b=STREAMS, h=DH)
        od_T = flat(w_uq)[:, 1024:1536].rearrange("p (h n) -> p h n", h=DH)
        lat_flat = lat[:, :, :].rearrange("p a b -> p (a b)")
        gains = lat_flat[:, 0:2 * D].rearrange("p (a b) -> p a b", a=2)
        caches = mlaK[:, :, :].rearrange("p a b -> p (a b)").rearrange("p (r c b n) -> p r c b n", r=2, c=2, b=2)
        dk_c, dv_c = caches[:, 0], caches[:, 1]
        dk_cT = vm[:, :, :].rearrange("p a b -> p (a b)").rearrange("p (s h k) -> p s h k", s=2, h=DH)
        sq = diffT[:, :, :, :].rearrange("p a b c -> p (a b c)")
        l0.close()

        l1 = ExitStack()
        kv = alloc(l1, "kv", [2, TILES, 2 * GW])
        kT = alloc(l1, "kT", [2, 2, TOK])
        qT1 = alloc(l1, "qT1", [2, 2, TOK])
        g1 = alloc(l1, "g1", [2, PT_TILES, GW])
        gsT = alloc(l1, "gsT", [2, 2, P])
        gtmp = alloc(l1, "gtmp", [2, 512])
        oT = alloc(l1, "oT", [KD, TOK])
        qblk1 = alloc(l1, "qblk1", [2, STREAMS, 2, GH * NEW])
        k_c = alloc(l1, "k_c", [4, 2, GW])
        v_c = alloc(l1, "v_c", [4, 2, GW])
        newv1 = alloc(l1, "newv1", [4, GW])
        k_cT = alloc(l1, "k_cT", [4, 2, PAST])
        soft = alloc(l1, "soft", [2, 512])
        cum = alloc(l1, "cum", [512])
        ones = alloc(l1, "ones", [512])
        gains1 = flat(xT)[:, 0:2 * D].rearrange("p (a b) -> p a b", a=2)
        l1.close()

        bank = {f"{r}{i}": ctx.enter_context(nc.psum_tensor(f"{r}{i}", [P, 512], F32))
                for r in BANKS for i in range(BANKS[r])}
        filled = {b: sem(f"filled_{b}") for b in bank}
        drained = {b: sem(f"drained_{b}") for b in bank}
        consts_in, small_in, xres_in = sem("consts_in"), sem("small_in"), sem("xres_in")
        x_in = [sem(f"x_in{t}") for t in range(TILES)]
        gains_in, gains1_in = sem("gains_in"), sem("gains1_in")
        w_in = [sem(f"w_in{i}") for i in range(3)]
        ckv_in = [sem(f"ckv_in{i}") for i in range(CKV_SLOTS)]
        kr_in, newckv_in = sem("kr_in"), sem("newckv_in")
        dk_in = [sem(f"dk_in{i}") for i in range(2)]
        dv_in = [sem(f"dv_in{i}") for i in range(2)]
        kc_in = [sem(f"kc_in{i}") for i in range(4)]
        vc_in = [sem(f"vc_in{i}") for i in range(4)]
        rms_done, uq_done, rot_done = sem("rms_done"), sem("uq_done"), sem("rot_done")
        setup_done = sem("setup_done")
        blocks_done = sem("blocks_done")
        max_done, weigh_done = sem("max_done"), sem("weigh_done")
        soft_done, stick_done = sem("soft_done"), sem("stick_done")
        dve_lam, act_lam = sem("dve_lam"), sem("act_lam")
        gate_e = sem("gate_e")
        pow_in, pow_out = sem("pow_in"), sem("pow_out")
        post_done, ln_done = sem("post_done"), sem("ln_done")
        dve_step, act_step, pool_step = sem("dve_step"), sem("act_step"), sem("pool_step")
        stored = sem("stored")
        stored_ckv, stored_dv = sem("stored_ckv"), sem("stored_dv")
        stored_v = [sem(f"stored_v{g}") for g in range(GROUPS)]
        stored_rot = [sem(f"stored_rot{i}") for i in range(2)]
        stored_kv = [sem(f"stored_kv{i}") for i in range(2)]

        def ps(job):
            return bank[where[job][0]]

        def wait_filled(eng, job):
            eng.wait_ge(filled[where[job][0]], where[job][1])

        def wait_drained(eng, job):
            eng.wait_ge(drained[where[job][0]], where[job][1])

        def wait_bank(eng, job):
            b, n = where[job]
            if n > 1:
                eng.wait_ge(drained[b], n - 1)

        def tok(t):
            return slice(t * P, (t + 1) * P)

        def new(b):
            return slice(SEQ + b * NEW, SEQ + (b + 1) * NEW)

        def ordinal(kinds, pick=lambda j: True):
            js = [j for j in schedule if j[0] in kinds and pick(j)]
            return {j: i + 1 for i, j in enumerate(js)}

        pow_no = ordinal(("rms", "post", "ln"))
        rot_no = ordinal(("dq", "dk"))
        post_no = ordinal(("post",))
        ln_no = ordinal(("ln",))
        gate_no = ordinal(("g", "gs"))
        blocks_no = ordinal(("qblocks", "gblocks"))
        exp_no = {s: i + 1 for i, s in enumerate(
            j for j in schedule if j[0] in ("score", "score2") and j[1][0] in ("M", "MS", "D", "DS"))}
        weigh_no = {s: i + 1 for i, s in enumerate(s for s in exp_steps if s[0] != "M")}
        stick_no = {s: i + 1 for i, s in enumerate(sb_steps)}

        def wcols(w, c0, n):
            return w.rearrange("(k p) c -> p k c", p=P)[:, :, c0:c0 + n]

        w0 = a["w_in_even"].rearrange("a k c -> (a k) c")
        w1 = a["w_in_odd"].rearrange("a k c -> (a k) c")
        wo = [a["w_out_even"].rearrange("a k c -> (a k) c"), a["w_out_odd"].rearrange("a k c -> (a k) c")]
        x_p = a["x_prompt"].rearrange("b (t p) d -> p (b t) d", p=P)
        x_s = a["x_sample"].rearrange("b q d -> (b q) d")
        ckv_cache = a["cache_mla_ckv"].rearrange("a b (h p) c -> p (a b) h c", p=P)
        kr_cache = a["cache_mla_krope"].rearrange("a b (h p) c -> p (a b h) c", p=P)
        dk_cache = a["cache_diff_k"].rearrange("a b (h p) n i d -> p (a b) h (n i d)", p=P)
        dv_cache = a["cache_diff_v"].rearrange("a b (h p) n d -> p (a b) h (n d)", p=P)
        sk_cache = a["cache_sb_k"].rearrange("a b (h p) n d -> p (a b) h (n d)", p=P)
        sv_cache = a["cache_sb_v"].rearrange("a b (h p) n d -> p (a b) h (n d)", p=P)
        y_p = out[0].rearrange("b (t p) d -> t p (b d)", p=P)
        y_s = out[1].rearrange("b q d -> (b q) d")
        ckv_p = out[2].rearrange("a b (t p) c -> p (a b t) c", p=P)
        kr_p = out[3].rearrange("a b (t p) c -> p (a b t) c", p=P)
        dk_p = out[4].rearrange("a b (t p) n i d -> t p (a b n i d)", p=P)
        dv_p = out[5].rearrange("a b (t p) n d -> t p (a b n d)", p=P)
        sk_p = out[6].rearrange("a b (t p) n d -> t p (a b n d)", p=P)
        sv_p = out[7].rearrange("a b (t p) n d -> t p (a b n d)", p=P)
        ckv_s = out[8].rearrange("a b q c -> (a b q) c")
        kr_s = out[9].rearrange("a b q c -> (a b q) c")
        dk_s = out[10].rearrange("a b q n i d -> (a b q) (n i d)")
        dv_s = out[11].rearrange("a b q n d -> (a b q) (n d)")
        sk_s = out[12].rearrange("a b q n d -> (a b q) (n d)")
        sv_s = out[13].rearrange("a b q n d -> (a b q) (n d)")

        block = ctx.enter_context(nc.Block())

        @block.sync
        def _(sp):
            C_Q, C_G0 = SEC_A + MLA_W, SEC_A
            for t in range(TILES):
                src = x_p[:, t, :] if t < PT_TILES else x_s
                sp.dma_start(x_sb[:, t, :], src).then_inc(x_in[t], 16)
                if t == 0:
                    sp.dma_start(ident[:, :], a["c_ident"]).then_inc(consts_in, 16)
            sp.dma_start(w_sb[:, 0, :, 0:SEC_A], wcols(w0, 0, SEC_A)).then_inc(w_in[0], 16)
            sp.dma_start(w_sb[:, 1, :, :], wcols(w0, C_G0, MLA_W)).then_inc(w_in[1], 16)
            sp.dma_start(probs[:, 0, 0:MASKS], a["c_masks"]).then_inc(small_in, 16)
            for buf, name in ((sel, "c_sel"), (sign, "c_sign")):
                sp.dma_start(buf[:, :], a[name]).then_inc(small_in, 16)
            sp.dma_start(ropem[:, :, :], a["c_ropem"]).then_inc(small_in, 16)
            sp.dma_start(roped[:, :, :], a["c_roped"]).then_inc(small_in, 16)
            for buf, src in ((g_q, a["q_norm_g"]), (g_kv, a["kv_norm_g"]), (g_sub, a["diff_subln_g"])):
                sp.dma_start(buf[:, :], src.rearrange("a c -> (a c)").partition_broadcast(P)).then_inc(small_in, 16)
            sp.dma_start(lam4[:, 0:2, :], a["diff_lambda_q"].rearrange("a i d -> (a i) d").partition_broadcast(P)).then_inc(small_in, 16)
            sp.dma_start(lam4[:, 2:4, :], a["diff_lambda_k"].rearrange("a i d -> (a i) d").partition_broadcast(P)).then_inc(small_in, 16)
            sp.dma_start(w_uq[:, :, :], a["w_uq"].rearrange("a (k p) c -> p (a k) c", p=P)).then_inc(small_in, 16)
            sp.dma_start(w_uk[:, :], a["w_uk"].rearrange("a c h n -> (a c) (h n)")).then_inc(small_in, 16)
            sp.dma_start(w_uv[:, :], a["w_uv"].rearrange("a c h n -> (a c) (h n)")).then_inc(small_in, 16)
            sp.dma_start(kr_c[:, 2 * ROT:].rearrange("p (b r) -> p b r", r=ROT), kr_cache).then_inc(kr_in, 16)
            for b in range(CKV_SLOTS):
                sp.dma_start(ckv_c[:, b, :, :], ckv_cache[:, b, :, :]).then_inc(ckv_in[b], 16)

            def load_diff_k(b):
                sp.dma_start(dk_c[:, b % 2, :, :], dk_cache[:, b, :, :]).then_inc(dk_in[b % 2], 16)

            def load_diff_v(b):
                sp.dma_start(dv_c[:, b % 2, :, :], dv_cache[:, b, :, :]).then_inc(dv_in[b % 2], 16)
                if b == 0:
                    sp.wait_ge(stored_dv, 16)
                sp.dma_start(newv[0:NEW, b % 2, :], dv_s[b * NEW:(b + 1) * NEW, :]).then_inc(dv_in[b % 2], 16)

            def load_stick_k(g, b):
                sp.dma_start(k_c[:, b % 4, :, :], sk_cache[:, b, :, g * GW:(g + 1) * GW]).then_inc(kc_in[b % 4], 16)

            def load_stick_v(g, b):
                sp.dma_start(v_c[:, b % 4, :, :], sv_cache[:, b, :, g * GW:(g + 1) * GW]).then_inc(vc_in[b % 4], 16)
                if b == 0:
                    sp.wait_ge(stored_v[g], 16)
                sp.dma_start(newv1[0:NEW, b % 4, :],
                             sv_s[b * NEW:(b + 1) * NEW, g * GW:(g + 1) * GW]).then_inc(vc_in[b % 4], 16)

            last_m = ("value", ("MS", STREAMS - 1))
            w_next = {("A", S_TILE): (0, w0, C_Q), ("G", S_TILE): (1, w0, C_Q + DIFF_W),
                      ("dq", S_TILE): (0, w0, C_Q + 2 * DIFF_W), ("dk", S_TILE): (1, w0, C_Q + 3 * DIFF_W),
                      ("dv", S_TILE): (0, wo[0], 0), ("gd", S_TILE): (1, wo[0], 512)}
            for job in schedule:
                kind = job[0]
                if job in w_next:
                    slot, w, c0 = w_next[job]
                    wait_filled(sp, job)
                    sp.dma_start(w_sb[:, slot, :, :], wcols(w, c0, 512)).then_inc(w_in[slot], 16)
                if kind == "latT" and job[1] == S_TILE:
                    sp.wait_ge(stored_ckv, 16 * 2)
                    sp.dma_start(newckv[0:NEW, :, :], out[8].rearrange("a b q c -> q (a b) c")).then_inc(newckv_in, 16)
                if kind == "value" and job[1][0] == "MS":
                    b = job[1][1]
                    wait_filled(sp, job)
                    if b + CKV_SLOTS < STREAMS:
                        sp.dma_start(ckv_c[:, b, :, :], ckv_cache[:, b + CKV_SLOTS, :, :]).then_inc(ckv_in[b], 16)
                if job == last_m:
                    for b in range(2):
                        load_diff_k(b)
                        load_diff_v(b)
                    for t in range(TILES):
                        src = x_p[:, t, :] if t < PT_TILES else x_s
                        sp.dma_start(x_sb[:, t, :], src).then_inc(xres_in, 16)
                if job == ("om",):
                    wait_filled(sp, job)
                    for i, name in enumerate(("ln_even_g", "ln_even_b")):
                        sp.dma_start(gains[:, i, :], a[name].rearrange("a c -> (a c)").partition_broadcast(P)).then_inc(gains_in, 16)
                if kind == "cacheT" and job[1] == "DS" and job[3] == 1 and job[2] + 2 < STREAMS:
                    wait_filled(sp, job)
                    load_diff_k(job[2] + 2)
                if kind == "value" and job[1][0] == "DS" and job[1][1] + 2 < STREAMS:
                    wait_filled(sp, job)
                    load_diff_v(job[1][1] + 2)
                if job == ("out", 0, S_TILE, 1):
                    wait_filled(sp, job)
                    sp.dma_start(w_sb[:, 1, :, 0:GW], wcols(w1, D, GW)).then_inc(w_in[1], 16)
                    sp.dma_start(w_sb[:, 1, :, GW:], wcols(w1, 2 * D, GW)).then_inc(w_in[1], 16)
                    sp.dma_start(w_sb[:, 0, :, 0:GW], wcols(w1, 0, GW)).then_inc(w_in[0], 16)
                    sp.dma_start(w_sb[:, 0, :, GW:], wcols(w1, 3 * D, GW)).then_inc(w_in[2], 16)
                if job == ("xT", 1, S_TILE, 1):
                    wait_drained(sp, job)
                    for b in range(4):
                        load_stick_k(0, b)
                if job == ("kT", 0, S_TILE):
                    for b in range(4):
                        load_stick_v(0, b)
                if kind == "kv" and job[2] == S_TILE:
                    wait_filled(sp, job)
                    g = job[1] + 1
                    if g < GROUPS:
                        sp.dma_start(w_sb[:, 1, :, 0:GW], wcols(w1, D + g * GW, GW)).then_inc(w_in[1], 16)
                        sp.dma_start(w_sb[:, 1, :, GW:], wcols(w1, 2 * D + g * GW, GW)).then_inc(w_in[1], 16)
                    else:
                        sp.dma_start(w_sb[:, 1, :, :], wcols(wo[1], 512, 512)).then_inc(w_in[1], 16)
                if kind == "qs" and job[1] + 1 < GROUPS:
                    wait_filled(sp, job)
                    sp.dma_start(w_sb[:, 0, :, 0:GW], wcols(w1, (job[1] + 1) * GW, GW)).then_inc(w_in[0], 16)
                if kind == "gs":
                    wait_filled(sp, job)
                    g = job[1] + 1
                    if g < GROUPS:
                        sp.dma_start(w_sb[:, 0, :, GW:], wcols(w1, 3 * D + g * GW, GW)).then_inc(w_in[2], 16)
                    else:
                        sp.dma_start(w_sb[:, 0, :, :], wcols(wo[1], 0, 512)).then_inc(w_in[0], 16)
                        for i, name in enumerate(("ln_odd_g", "ln_odd_b")):
                            sp.dma_start(gains1[:, i, :], a[name].rearrange("a c -> (a c)").partition_broadcast(P)).then_inc(gains1_in, 16)
                if kind == "cacheT" and job[1] == "BS":
                    g, b = job[2], 2 * job[3] + job[4]
                    g, b = (g, b + 4) if b + 4 < STREAMS else (g + 1, b + 4 - STREAMS)
                    if g < GROUPS:
                        wait_filled(sp, job)
                        load_stick_k(g, b)
                if kind == "value" and job[1][0] == "BS":
                    for i in range(2):
                        g, b = job[1][1], 2 * job[1][2] + i
                        g, b = (g, b + 4) if b + 4 < STREAMS else (g + 1, b + 4 - STREAMS)
                        if g < GROUPS:
                            wait_filled(sp, job)
                            load_stick_v(g, b)

        @block.gpsimd
        def _(pool):
            nc.gpsimd.memset(minus_half[:, :], -0.5).then_inc(pool_step, 1)
            pool.wait_ge(pool_step, 1)
            total = 0
            for job in schedule:
                kind = job[0]
                if kind == "rms":
                    pool.wait_ge(pow_in, pow_no[job])
                    nc.gpsimd.tensor_tensor(ss[:, 2, :], ss[:, 1, :], minus_half[:, :], ALU.pow).then_inc(pow_out, 1)
                    pool.wait_ge(rms_done, 1)
                    pool.dma_start(ckv_s, lat[:, S_TILE, QL:QL + KVL]).then_inc(stored_ckv, 16)
                    pool.dma_start(kr_s, lat[:, S_TILE, QL + KVL:]).then_inc(stored_ckv, 16)
                    pool.wait_ge(stored_ckv, 32)
                    pool.dma_start(ckv_p, lat[:, 0:PT_TILES, QL:QL + KVL]).then_inc(stored_ckv, 16)
                    pool.dma_start(kr_p, lat[:, 0:PT_TILES, QL + KVL:]).then_inc(stored_ckv, 16)
                elif kind == "dk":
                    t = job[1]
                    pool.wait_ge(rot_done, rot_no[job])
                    pool.dma_start(dk_p[t] if t < PT_TILES else dk_s,
                                   rot[:, (rot_no[job] - 1) % 2, :]).then_inc(stored_rot[(rot_no[job] - 1) % 2], 16)
                elif kind == "dv":
                    t = job[1]
                    wait_drained(pool, job)
                    if t < PT_TILES:
                        total += 16
                        pool.dma_start(dv_p[t], dv[:, t, :]).then_inc(stored, 16)
                    else:
                        pool.dma_start(dv_s, dv[:, t, :]).then_inc(stored_dv, 16)
                elif kind == "post":
                    pool.wait_ge(pow_in, pow_no[job])
                    nc.gpsimd.tensor_tensor(ss[:, 2, 0:DH], ss[:, 1, 0:DH], minus_half[:, 0:DH], ALU.pow).then_inc(pow_out, 1)
                elif kind == "ln":
                    pool.wait_ge(pow_in, pow_no[job])
                    nc.gpsimd.tensor_tensor(rstd[:, :], mv[:, 1:2], minus_half[:, 0:1], ALU.pow).then_inc(pow_out, 1)
                    if job[1] == 1:
                        t = job[2]
                        pool.wait_ge(ln_done, ln_no[job])
                        total += 16
                        pool.dma_start(y_p[t] if t < PT_TILES else y_s, x_sb[:, t, :]).then_inc(stored, 16)
                elif kind == "kv":
                    _, g, t = job
                    wait_drained(pool, job)
                    cols = slice(g * GW, (g + 1) * GW)
                    dk_, dv_ = (sk_p[t], sv_p[t]) if t < PT_TILES else (sk_s, sv_s)
                    pool.dma_start(dk_[:, cols], kv[:, g % 2, t, 0:GW]).then_inc(stored_kv[g % 2], 16)
                    pool.dma_start(dv_[:, cols], kv[:, g % 2, t, GW:]).then_inc(
                        stored_kv[g % 2] if t < PT_TILES else stored_v[g], 16)
            pool.wait_ge(stored, total)
            pool.wait_ge(stored_ckv, 64)
            pool.wait_ge(stored_dv, 16)
            for g in range(GROUPS):
                pool.wait_ge(stored_v[g], 16)
            for i in range(2):
                pool.wait_ge(stored_kv[i], 16 * (2 * TILES - 1) * GROUPS // 2)
            pool.wait_ge(stored_rot[0], 16 * 2)
            pool.wait_ge(stored_rot[1], 16 * 3)

        @block.tensor
        def _(pe):
            def mm(o, l, r, first, last):
                return nc.tensor.matmul(o, l, r, start=first, stop=last)

            def project(job, slot, c0, n, t, src=xT, ks=range(KD)):
                wait_bank(pe, job)
                for k in ks:
                    i = mm(ps(job)[:, 0:n], src[:, k, tok(t)], w_sb[:, slot, k, c0:c0 + n], k == ks[0], k == ks[-1])
                i.then_inc(filled[where[job][0]], 1)

            def transposes(job, pieces):
                wait_bank(pe, job)
                for c0, src in pieces:
                    r, c = src.shape
                    i = nc.tensor.transpose(ps(job)[0:c, c0:c0 + r], src, ident[0:r, 0:r])
                i.then_inc(filled[where[job][0]], 1)

            pe.wait_ge(consts_in, 16)
            for job in schedule:
                kind = job[0]
                done = filled[where[job][0]] if job in where else None
                if kind == "xT":
                    _, layer, t, h = job
                    if layer == 0:
                        pe.wait_ge(x_in[t], 16)
                    else:
                        pe.wait_ge(ln_done, ln_no[("ln", 0, t)])
                    transposes(job, [(i * P, x_sb[:, t, (4 * h + i) * P:(4 * h + i + 1) * P]) for i in range(4)])
                elif kind == "A":
                    if job[1] == 0:
                        pe.wait_ge(w_in[0], 16)
                    for h in range(2):
                        wait_drained(pe, ("xT", 0, job[1], h))
                    project(job, 0, 0, SEC_A, job[1])
                elif kind in ("G", "dq", "dk", "dv", "gd"):
                    slot, n = {"G": (1, 1), "dq": (0, 2), "dk": (1, 2), "dv": (0, 3), "gd": (1, 3)}[kind]
                    pe.wait_ge(w_in[slot], 16 * n)
                    project(job, slot, 0, 512, job[1])
                elif kind == "latT":
                    t = job[1]
                    pe.wait_ge(rms_done, 1)
                    transposes(job, [(0, lat[:, t, 0:P]), (P, lat[:, t, P:2 * P]), (2 * P, lat[:, t, QL:QL + KVL]),
                                     (3 * P, lat[:, t, SEC_A - QK:SEC_A])])
                elif kind == "uq":
                    _, t, h = job
                    wait_drained(pe, ("latT", t))
                    pe.wait_ge(small_in, 16 * SMALL)
                    wait_bank(pe, job)
                    n = MH * QK // 2
                    for k in range(2):
                        i = mm(ps(job)[:, 0:n], latT[:, k, tok(t)], w_uq[:, k, h * n:(h + 1) * n], k == 0, k == 1)
                    i.then_inc(done, 1)
                elif kind == "qT":
                    _, t, h = job
                    pe.wait_ge(uq_done, t + 1)
                    transposes(job, [(i * P, uq[:, t % 2, (4 * h + i) * QK:(4 * h + i + 1) * QK]) for i in range(4)])
                elif kind == "kn":
                    h = job[1]
                    for t in range(PT_TILES):
                        wait_drained(pe, ("latT", t))
                    wait_bank(pe, job)
                    mm(ps(job)[0:NOPE, :], w_uk[:, h * NOPE:(h + 1) * NOPE], latT[:, 2, 0:SEQ], True, True).then_inc(done, 1)
                elif kind == "vm":
                    wait_bank(pe, job)
                    mm(ps(job)[:, :], latT[:, 2, tok(job[1])], w_uv[:, :], True, True).then_inc(done, 1)
                elif kind == "wukT":
                    transposes(job, [(i * P, w_uk[:, (4 * job[1] + i) * NOPE:(4 * job[1] + i + 1) * NOPE]) for i in range(4)])
                elif kind == "qa":
                    wait_drained(pe, ("wukT", job[1]))
                    wait_drained(pe, ("qT", S_TILE, job[1]))
                    wait_bank(pe, job)
                    for i in range(4):
                        h = 4 * job[1] + i
                        m = mm(ps(job)[:, i * P:(i + 1) * P], wukT[0:NOPE, h, :], qT[0:NOPE, h, tok(S_TILE)], True, True)
                    m.then_inc(done, 1)
                elif kind in ("dqT", "dkT"):
                    n = rot_no[(kind[:2], job[1])]
                    pe.wait_ge(rot_done, n)
                    transposes(job, [(i * P, rot[:, (n - 1) % 2, i * P:(i + 1) * P]) for i in range(4)])
                elif kind == "cacheT" and job[1] == "MS":
                    b = job[2]
                    pe.wait_ge(ckv_in[b % CKV_SLOTS], 16 * (b // CKV_SLOTS + 1))
                    pe.wait_ge(kr_in, 16)
                    pe.wait_ge(setup_done, 1)
                    wait_bank(pe, job)
                    for i in range(2):
                        nc.tensor.transpose(ps(job)[:, i * P:(i + 1) * P], ckv_c[:, b % CKV_SLOTS, i, :], ident[:, :])
                    for i in range(2):
                        m = nc.tensor.transpose(ps(job)[0:QK, (2 + i) * P:(3 + i) * P],
                                                kr_c[:, (2 * b + i) * ROT:(2 * b + i + 3) * ROT], ident[:, :])
                    m.then_inc(done, 1)
                elif kind == "cacheT" and job[1] == "DS":
                    b, half = job[2], job[3]
                    pe.wait_ge(dk_in[b % 2], 16 * (b // 2 + 1))
                    transposes(job, [(i * P, dk_c[:, b % 2, half, i * P:(i + 1) * P]) for i in range(4)])
                elif kind == "cacheT":
                    g, b = job[2], 2 * job[3] + job[4]
                    pe.wait_ge(kc_in[b % 4], 16 * (2 * g + b // 4 + 1))
                    transposes(job, [((2 * i + half) * P, k_c[:, b % 4, half, i * P:(i + 1) * P])
                                     for i in range(2) for half in range(2)])
                elif kind in ("score", "score2"):
                    s = job[1]
                    n = width(s)
                    wait_bank(pe, job)
                    o = ps(job)
                    if s[0] == "M":
                        _, t, h = s
                        for j in range(4):
                            wait_drained(pe, ("kn", h))
                            wait_drained(pe, ("latT", j))
                        for i in range(2):
                            wait_drained(pe, ("qT", t, i))
                        mm(o[:, 0:n], qT[0:QK, h, tok(t)], mlaK[0:QK, h, 0:n], True, False)
                        mm(o[:, n - P:n], identb[:, :], mask_chunk[:, :], False, True).then_inc(done, 1)
                    elif s[0] == "MS":
                        b = s[1]
                        wait_drained(pe, ("cacheT",) + s)
                        for i in range(2):
                            wait_drained(pe, ("qa", i))
                        qn, qrb = qa[:, b, :], qr[NOPE:QK, b, :]
                        mm(o[:, 0:PAST], qn, ckv_cT[:, b % 2, :], True, False)
                        mm(o[:, 0:PAST], qrb, kr_cT[NOPE:QK, b % 2, :], False, True)
                        mm(o[:, PAST:n], qn, ckvTs[:, b * NEW:(b + 1) * NEW], True, False)
                        mm(o[:, PAST:n], qrb, krTs[NOPE:QK, b * NEW:(b + 1) * NEW], False, True).then_inc(done, 1)
                    elif s[0] == "D":
                        _, t, h = s
                        r = slice(HD * (kind == "score2"), HD * (kind == "score2") + HD)
                        for j in range(t + 1):
                            wait_drained(pe, ("dkT", j))
                        wait_drained(pe, ("dqT", t))
                        mm(o[:, 0:n], diffT[r, 0, h, tok(t)], diffT[r, 1, h, 0:n], True, False)
                        mm(o[:, n - P:n], identb[:, :], mask_chunk[:, :], False, True).then_inc(done, 1)
                    elif s[0] == "DS":
                        b = s[1]
                        for i in range(2):
                            wait_drained(pe, ("cacheT",) + s + (i,))
                        wait_drained(pe, ("dkT", S_TILE))
                        pe.wait_ge(blocks_done, blocks_no[("qblocks",)])
                        for h in range(DH):
                            r = slice(2 * NEW * h, 2 * NEW * (h + 1))
                            mm(o[r, 0:PAST], qblk[:, b, h, :], dk_cT[:, b % 2, h, :], True, True)
                            m = mm(o[r, PAST:n], qblk[:, b, h, :], diffT[:, 1, h, new(b)], True, True)
                        m.then_inc(done, 1)
                    elif s[0] == "B":
                        _, g, t, h = s
                        r = slice(HD * (h % 2), HD * (h % 2) + HD)
                        for j in range(t + 1):
                            wait_drained(pe, ("kT", g, j))
                        wait_drained(pe, ("q", g, h // 2))
                        mm(o[:, 0:n], qT1[r, g % 2, h // 2, tok(t)], kT[r, g % 2, h // 2, 0:n], True, False)
                        mm(o[:, n - P:n], identb[:, :], mask_causal[:, :], False, True).then_inc(done, 1)
                    else:
                        _, g, pair = s
                        wait_drained(pe, ("kT", g, S_TILE))
                        pe.wait_ge(blocks_done, blocks_no[("gblocks", g)])
                        for i in range(2):
                            b = 2 * pair + i
                            wait_drained(pe, ("cacheT",) + s + (i,))
                            r = slice(GH * NEW * i, GH * NEW * (i + 1))
                            for blk in range(2):
                                mm(o[r, 0:PAST], qblk1[:, g % 2, b, blk, :], k_cT[:, b % 4, blk, :], blk == 0, blk == 1)
                            for blk in range(2):
                                mm(o[r, PAST:n], qblk1[:, g % 2, b, blk, :], kT[:, g % 2, blk, new(b)], blk == 0, False)
                            m = mm(o[r, PAST:n], identb[:, r], mask_new[:, :], False, True)
                        m.then_inc(done, 1)
                elif kind == "turn":
                    s = job[1]
                    wait_bank(pe, job)
                    if s[0] == "M":
                        wait_drained(pe, ("score", s))
                    elif s in weigh_no:
                        pe.wait_ge(weigh_done, weigh_no[s])
                    else:
                        pe.wait_ge(stick_done, stick_no[s])
                    p = probs[:, nth[s] % 3, :]
                    for j, (k0, kn) in enumerate(turn_blocks(s)):
                        if s[0] == "DS":
                            m = mm(ps(job)[0:kn, j * DIFF_ROWS:(j + 1) * DIFF_ROWS], p[:, k0:k0 + kn],
                                   csel[:, s[1] % 2, :], True, True)
                        else:
                            m = nc.tensor.transpose(ps(job)[0:kn, j * P:(j + 1) * P], p[:, k0:k0 + kn], ident[:, :])
                    m.then_inc(done, 1)
                elif kind == "value":
                    s = job[1]
                    wait_bank(pe, job)
                    wait_drained(pe, ("turn", s))
                    o, w = ps(job), wT[:, nth[s] % 2, :]
                    blocks = turn_blocks(s)
                    last = len(blocks) - 1
                    if s[0] == "M":
                        h = s[2]
                        for j in range(last + 1):
                            wait_drained(pe, ("vm", j))
                            m = mm(o[:, 0:MV], w[:, tok(j)], vm[:, j, h * MV:(h + 1) * MV], j == 0, j == last)
                    elif s[0] == "MS":
                        b = s[1]
                        pe.wait_ge(newckv_in, 16)
                        for j in range(2):
                            mm(o[:, 0:P], ckv_c[:, b % CKV_SLOTS, j, :], w[:, tok(j)], j == 0, False)
                        m = mm(o[:, 0:P], newckv[0:NEW, b, :], w[0:NEW, tok(2)], False, True)
                    elif s[0] == "D":
                        h = s[2]
                        for j in range(last + 1):
                            wait_drained(pe, ("dv", j))
                            m = mm(o[:, 0:P], w[:, tok(j)], dv[:, j, h * P:(h + 1) * P], j == 0, j == last)
                    elif s[0] == "DS":
                        b = s[1]
                        pe.wait_ge(dv_in[b % 2], 32 * (b // 2 + 1))
                        for h in range(DH):
                            c = slice(h * NEW, (h + 1) * NEW)
                            hc = slice(h * P, (h + 1) * P)
                            for j in range(2):
                                mm(o[:, c], dv_c[:, b % 2, j, hc], w[:, j * DIFF_ROWS + h * NEW:j * DIFF_ROWS + (h + 1) * NEW], j == 0, False)
                            m = mm(o[:, c], newv[0:NEW, b % 2, hc],
                                   w[0:NEW, 2 * DIFF_ROWS + h * NEW:2 * DIFF_ROWS + (h + 1) * NEW], False, True)
                    elif s[0] == "B":
                        _, g, t, h = s
                        for j in range(last + 1):
                            m = mm(o[:, 0:HD], w[:, tok(j)], kv[:, g % 2, j, GW + h * HD:GW + (h + 1) * HD], j == 0, j == last)
                    else:
                        _, g, pair = s
                        for i in range(2):
                            b = 2 * pair + i
                            pe.wait_ge(vc_in[b % 4], 32 * (2 * g + b // 4 + 1))
                            for blk in range(2):
                                c0 = (2 * i + blk) * 2 * NEW
                                oc, vc = o[:, c0:c0 + 2 * NEW], slice(blk * P, (blk + 1) * P)
                                for j in range(2):
                                    mm(oc, v_c[:, b % 4, j, vc], w[:, j * P + c0:j * P + c0 + 2 * NEW], j == 0, False)
                                m = mm(oc, newv1[0:NEW, b % 4, vc], w[0:NEW, 2 * P + c0:2 * P + c0 + 2 * NEW], False, True)
                    m.then_inc(done, 1)
                elif kind == "om":
                    wait_drained(pe, ("value", ("MS", STREAMS - 1)))
                    wait_bank(pe, job)
                    for h in range(MH):
                        m = mm(ps(job)[:, h * MV:(h + 1) * MV], o_mlaT[:, h, :], w_uv[:, h * MV:(h + 1) * MV], True, True)
                    m.then_inc(done, 1)
                elif kind == "od":
                    wait_drained(pe, ("value", ("DS", STREAMS - 1)))
                    transposes(job, [(h * P, od_T[:, h, :]) for h in range(DH)])
                elif kind == "ogT":
                    _, t, h = job
                    if h == 0:
                        wait_drained(pe, ("value", ("M", t, MH - 1)) if t < PT_TILES else ("om",))
                    else:
                        pe.wait_ge(post_done, post_no[("post", t)])
                    transposes(job, [(i * P, gates[:, t, (4 * h + i) * P:(4 * h + i + 1) * P]) for i in range(4)])
                elif kind in ("outp", "out"):
                    _, layer, t, h = job
                    early = 4 if layer == 0 else 2 * (GROUPS - 1)
                    ks = range(early) if kind == "outp" else range(early, KD)
                    if layer == 0:
                        wait_drained(pe, ("ogT", t, int(kind == "out")))
                        pe.wait_ge(w_in[h], 16 * 4)
                    else:
                        for g in range(GROUPS - 1) if kind == "outp" else [GROUPS - 1]:
                            wait_drained(pe, ("oT", g, t) if t < PT_TILES else ("value", ("BS", g, STREAMS // 2 - 1)))
                        pe.wait_ge(w_in[h], 16 * (5 + GROUPS) if h == 0 else 16 * (5 + 2 * GROUPS))
                    project(job, h, 0, 512, t, xT if layer == 0 else oT, ks)
                elif kind == "kv":
                    _, g, t = job
                    pe.wait_ge(w_in[1], 16 * (6 + 2 * g))
                    for h in range(2):
                        wait_drained(pe, ("xT", 1, t, h))
                    project(job, 1, 0, 2 * GW, t)
                elif kind == "kT":
                    _, g, t = job
                    wait_drained(pe, ("kv", g, t))
                    transposes(job, [(i * P, kv[:, g % 2, t, i * P:(i + 1) * P]) for i in range(2)])
                elif kind in ("q", "qs", "gs"):
                    g = job[1]
                    if kind == "gs":
                        pe.wait_ge(w_in[2], 16 * (g + 1))
                    else:
                        pe.wait_ge(w_in[0], 16 * (5 + g))
                    wait_bank(pe, job)
                    c = GW if kind == "gs" else 0
                    if kind == "q":
                        blocks, cols, n = [job[2]], slice(0, SEQ), SEQ
                    else:
                        blocks, cols, n = [0, 1], tok(S_TILE), P
                    for i, blk in enumerate(blocks):
                        for k in range(KD):
                            m = mm(ps(job)[:, i * n:(i + 1) * n], w_sb[:, 0, k, c + blk * P:c + (blk + 1) * P],
                                   xT[:, k, cols], k == 0, k == KD - 1)
                    m.then_inc(done, 1)
                elif kind == "g":
                    pe.wait_ge(w_in[2], 16 * (job[1] + 1))
                    project(job, 0, GW, GW, job[2])
                elif kind == "oT":
                    _, g, t = job
                    wait_drained(pe, ("value", ("B", g, t, GH - 1)))
                    transposes(job, [(i * P, g1[:, g % 2, t, i * P:(i + 1) * P]) for i in range(2)])

        @block.scalar
        def _(act):
            steps_done = [0]

            def link(ins):
                steps_done[0] += 1
                ins.then_inc(act_step, 1)
                act.wait_ge(act_step, steps_done[0])

            for job in schedule:
                kind = job[0]
                done = drained[where[job][0]] if job in where else None
                if kind == "xT" and job[3] == 1:
                    wait_filled(act, job)
                    nc.scalar.copy(xT[:, 4:8, tok(job[2])], ps(job)[:, :].rearrange("p (k n) -> p k n", k=4)).then_inc(done, 1)
                elif kind == "A":
                    wait_filled(act, job)
                    nc.scalar.copy(lat[:, job[1], :], ps(job)[:, 0:SEC_A]).then_inc(done, 1)
                elif kind in ("G", "gd"):
                    wait_filled(act, job)
                    c0 = MLA_W * (kind == "gd")
                    nc.scalar.activation(gates[:, job[1], c0:c0 + 512], ps(job)[:, :], ACT.Silu).then_inc(done, 1)
                elif kind == "uq":
                    _, t, h = job
                    wait_filled(act, job)
                    n = MH * QK // 2
                    nc.scalar.copy(uq[:, t % 2, h * n:(h + 1) * n], ps(job)[:, 0:n]).then_inc(done, 1)
                elif kind == "qT":
                    _, t, h = job
                    wait_filled(act, job)
                    nc.scalar.mul(qT[0:QK, 4 * h:4 * h + 4, tok(t)],
                                  ps(job)[0:QK, :].rearrange("p (k n) -> p k n", k=4), MLA_SCALE).then_inc(done, 1)
                elif kind == "vm":
                    wait_filled(act, job)
                    nc.scalar.copy(vm[:, job[1], :], ps(job)[:, :]).then_inc(done, 1)
                elif kind == "qa":
                    wait_filled(act, job)
                    half = slice(4 * job[1] * NEW, 4 * (job[1] + 1) * NEW)
                    nc.scalar.copy(qr[NOPE:QK, :, half].rearrange("p b (h q) -> p h b q", h=4),
                                   qT[NOPE:QK, 4 * job[1]:4 * job[1] + 4, tok(S_TILE)].rearrange("p h (b q) -> p h b q", q=NEW))
                    nc.scalar.copy(qa[:, :, half].rearrange("p b (h q) -> p h b q", h=4),
                                   ps(job)[:, :].rearrange("p (h b q) -> p h b q", h=4, q=NEW)).then_inc(done, 1)
                elif kind in ("dq", "dk"):
                    n = rot_no[job] - 1
                    wait_filled(act, job)
                    if kind == "dk" and n >= 7:
                        act.wait_ge(stored_rot[n % 2], 16 * ((n - 5) // 2))
                    nc.scalar.copy(rot[:, n % 2, :], ps(job)[:, :]).then_inc(done, 1)
                elif kind == "dqT":
                    wait_filled(act, job)
                    nc.scalar.mul(diffT[:, 0, :, tok(job[1])],
                                  ps(job)[:, :].rearrange("p (k n) -> p k n", k=4), HEAD_SCALE).then_inc(done, 1)
                elif kind == "dv":
                    wait_filled(act, job)
                    nc.scalar.copy(dv[:, job[1], :], ps(job)[:, :]).then_inc(done, 1)
                elif kind == "cacheT" and job[1] == "DS" or kind == "cacheT" and job[1] == "BS" and job[4] == 0:
                    wait_filled(act, job)
                    src = ps(job)[:, :].rearrange("p (k n) -> p k n", k=4)
                    if job[1] == "DS":
                        nc.scalar.copy(dk_cT[:, job[2] % 2, :, tok(job[3])], src).then_inc(done, 1)
                    else:
                        nc.scalar.copy(k_cT[:, (2 * job[3]) % 4, :, :].rearrange("p a b -> p (a b)"), ps(job)[:, :]).then_inc(done, 1)
                elif kind in ("score", "score2") and ("score", job[1]) in exp_no:
                    s = job[1]
                    act.wait_ge(max_done, exp_no[job])
                    r = nth[s] % 8
                    p, st = (probs[:, nth[s] % 3, :], stats) if kind == "score" else (probs2[:, nth[s] % 2, :], stats2)
                    nc.scalar.activation(p[:, 0:width(s)], ps(job)[:, 0:width(s)], ACT.Exp, bias=st[:, 0, r:r + 1],
                                         accum_out=st[:, 1, r:r + 1]).then_inc(done, 1)
                elif kind == "score":
                    s = job[1]
                    e = soft[:, nth[s] % 2, 0:width(s)]
                    wait_filled(act, job)
                    link(nc.scalar.activation(e, ps(job)[:, 0:width(s)], ACT.Abs))
                    link(nc.scalar.activation(e, e, ACT.Exp, scale=-1.0))
                    nc.scalar.activation(e, e, ACT.Ln, bias=1.0).then_inc(soft_done, 1)
                elif kind == "weigh" and job[1] in stick_no:
                    s = job[1]
                    p = probs[:, nth[s] % 3, 0:width(s)]
                    wait_drained(act, ("score", s))
                    nc.scalar.activation(p, p, ACT.Exp).then_inc(stick_done, 1)
                elif kind == "value" and job[1][0] in ("MS", "DS", "D"):
                    s = job[1]
                    wait_filled(act, job)
                    if s[0] == "MS":
                        nc.scalar.copy(o_mlaT[:, :, s[1] * NEW:(s[1] + 1) * NEW],
                                       ps(job)[:, 0:P].rearrange("p (h q) -> p h q", h=MH)).then_inc(done, 1)
                    elif s[0] == "DS":
                        nc.scalar.copy(od_T[:, :, s[1] * NEW:(s[1] + 1) * NEW],
                                       ps(job)[:, 0:DIFF_ROWS].rearrange("p (h q) -> p h q", h=DH)).then_inc(done, 1)
                    else:
                        _, t, h = s
                        if h == 0 and t < 2:
                            act.wait_ge(stored_rot[t], 16 * (2 + t))
                        elif h == 0:
                            act.wait_ge(post_done, t - 1)
                        nc.scalar.copy(rot[:, t % 2, h * P:(h + 1) * P], ps(job)[:, 0:P]).then_inc(done, 1)
                elif kind == "od":
                    wait_filled(act, job)
                    nc.scalar.copy(rot[:, S_TILE % 2, :], ps(job)[:, :]).then_inc(done, 1)
                elif kind == "ogT":
                    _, t, h = job
                    wait_filled(act, job)
                    nc.scalar.copy(xT[:, 4 * h:4 * h + 4, tok(t)], ps(job)[:, :].rearrange("p (k n) -> p k n", k=4)).then_inc(done, 1)
                elif kind == "rms":
                    act.wait_ge(dve_lam, 1)
                    nc.scalar.activation(lam[:, 2:4], lam[:, 0:2], ACT.Exp).then_inc(act_lam, 1)
                elif kind == "kv":
                    _, g, t = job
                    if g == 0 and t == 0:
                        nc.scalar.preload_act_table_set("natural_log_exp_and_others")
                    wait_filled(act, job)
                    if g >= 2 and t == 0:
                        act.wait_ge(stored_kv[g % 2], 16 * (2 * TILES - 1) * (g // 2))
                        act.wait_ge(stored_v[g - 2], 16)
                    nc.scalar.copy(kv[:, g % 2, t, :], ps(job)[:, :]).then_inc(done, 1)
                elif kind in ("q", "qs"):
                    g = job[1]
                    wait_filled(act, job)
                    if kind == "q":
                        nc.scalar.mul(qT1[:, g % 2, job[2], 0:SEQ], ps(job)[:, :], HEAD_SCALE).then_inc(done, 1)
                    else:
                        nc.scalar.mul(qT1[:, g % 2, :, tok(S_TILE)],
                                      ps(job)[:, 0:2 * P].rearrange("p (k n) -> p k n", k=2), HEAD_SCALE).then_inc(done, 1)
                elif kind in ("g", "gs"):
                    wait_filled(act, job)
                    nc.scalar.activation(gtmp[:, gate_no[job] % 2, 0:GW], ps(job)[:, 0:GW], ACT.Exp, scale=-1.0).then_inc(gate_e, 1)

        @block.vector
        def _(dve):
            v = nc.vector
            steps_done = [0]

            def link(ins):
                steps_done[0] += 1
                ins.then_inc(dve_step, 1)
                dve.wait_ge(dve_step, steps_done[0])

            def rotate(x1, x2, cos, sin, t1, t2):
                v.tensor_tensor(t1, x1, sin, ALU.mult)
                link(v.tensor_tensor(t2, x2, sin, ALU.mult))
                v.tensor_tensor(x1, x1, cos, ALU.mult)
                link(v.tensor_tensor(x2, x2, cos, ALU.mult))
                link(v.tensor_tensor(x1, x1, t2, ALU.subtract))
                return v.tensor_tensor(x2, x2, t1, ALU.add)

            v.memset(kr_c[:, 0:2 * ROT], 0.0).then_inc(setup_done, 1)
            for job in schedule:
                kind = job[0]
                done = drained[where[job][0]] if job in where else None
                if kind == "xT" and job[3] == 0:
                    wait_filled(dve, job)
                    v.tensor_copy(xT[:, 0:4, tok(job[2])], ps(job)[:, :].rearrange("p (k n) -> p k n", k=4)).then_inc(done, 1)
                elif kind == "rms":
                    dve.wait_ge(small_in, 16 * SMALL)
                    dve.wait_ge(consts_in, 16)
                    v.tensor_copy(identb[:, :], ident[:, :])
                    v.tensor_copy(mask_chunk[:, :], probs[:, 0, 0:P])
                    v.tensor_copy(mask_causal[:, :], probs[:, 0, P:2 * P])
                    v.tensor_copy(mask_new[:, :], probs[:, 0, 2 * P:MASKS])
                    link(v.tensor_tensor(lam4[:, 0:2, :], lam4[:, 0:2, :], lam4[:, 2:4, :], ALU.mult))
                    v.tensor_reduce(lam[:, 0:2], lam4[:, 0:2, :], AX_X, ALU.add).then_inc(dve_lam, 1)
                    for t in range(TILES):
                        wait_drained(dve, ("A", t))
                    q_, c_ = lat[:, :, 0:QL], lat[:, :, QL:QL + KVL]
                    sq_q = sq[:, 0:TILES * QL].rearrange("p (t c) -> p t c", t=TILES)
                    sq_c = sq[:, TILES * QL:TILES * (QL + KVL)].rearrange("p (t c) -> p t c", t=TILES)
                    v.tensor_tensor(sq_q, q_, q_, ALU.mult)
                    link(v.tensor_tensor(sq_c, c_, c_, ALU.mult))
                    v.tensor_reduce(ss[:, 0, 0:TILES], sq_q, AX_X, ALU.add)
                    link(v.tensor_reduce(ss[:, 0, TILES:], sq_c, AX_X, ALU.add))
                    v.tensor_scalar(ss[:, 1, 0:TILES], ss[:, 0, 0:TILES], 1.0 / QL, EPS, ALU.mult, ALU.add)
                    v.tensor_scalar(ss[:, 1, TILES:], ss[:, 0, TILES:], 1.0 / KVL, EPS, ALU.mult, ALU.add).then_inc(pow_in, 1)
                    dve.wait_ge(act_lam, 1)
                    link(v.tensor_tensor(lam[:, 4:5], lam[:, 3:4], lam[:, 2:3], ALU.subtract))
                    link(v.tensor_scalar(lam[:, 5:6], lam[:, 4:5], -LAM_INIT, None, ALU.add))
                    link(v.tensor_scalar(sign[:, 1:2], sign[:, 1:2], lam[:, 5:6], None, ALU.mult))
                    link(v.tensor_tensor(sign[:, 0:1], sign[:, 0:1], sign[:, 1:2], ALU.add))
                    link(v.tensor_scalar(g_sub[:, :], g_sub[:, :], 1.0 - LAM_INIT, None, ALU.mult))
                    dve.wait_ge(pow_out, pow_no[job])
                    v.tensor_tensor(q_, q_, ss[:, 2, 0:TILES].unsqueeze(2).broadcast_to([P, TILES, QL]), ALU.mult)
                    link(v.tensor_tensor(c_, c_, ss[:, 2, TILES:].unsqueeze(2).broadcast_to([P, TILES, KVL]), ALU.mult))
                    v.tensor_tensor(q_, q_, g_q[:, :].unsqueeze(1).broadcast_to([P, TILES, QL]), ALU.mult)
                    v.tensor_tensor(c_, c_, g_kv[:, :].unsqueeze(1).broadcast_to([P, TILES, KVL]), ALU.mult)
                    half = ROT // 2
                    k_ = lat[:, :, QL + KVL:]
                    t1 = sq[:, 3000:3000 + TILES * half].rearrange("p (t c) -> p t c", t=TILES)
                    t2 = sq[:, 3100:3100 + TILES * half].rearrange("p (t c) -> p t c", t=TILES)
                    rotate(k_[:, :, 0:half], k_[:, :, half:], ropem[:, :, 0:half], ropem[:, :, half:], t1, t2).then_inc(rms_done, 1)
                elif kind == "latT":
                    t = job[1]
                    wait_filled(dve, job)
                    v.tensor_copy(latT[:, :, tok(t)], ps(job)[:, 0:3 * P].rearrange("p (k n) -> p k n", k=3))
                    kr = ps(job)[NOPE:QK, 3 * P:]
                    if t < PT_TILES:
                        v.tensor_copy(mlaK[NOPE:QK, :, tok(t)], kr.unsqueeze(1).broadcast_to([ROT, MH, P])).then_inc(done, 1)
                    else:
                        v.tensor_copy(ckvTs[:, :], ps(job)[:, 2 * P:3 * P])
                        v.tensor_copy(krTs[NOPE:QK, :], kr).then_inc(done, 1)
                elif kind == "uqrope":
                    t = job[1]
                    for h in range(2):
                        wait_drained(dve, ("uq", t, h))
                    if t:
                        dve.wait_ge(uq_done, t)
                    q_ = uq[:, t % 2, :].rearrange("p (h c) -> p h c", h=MH)
                    half = ROT // 2
                    cos = ropem[:, t:t + 1, 0:half].broadcast_to([P, MH, half])
                    sin = ropem[:, t:t + 1, half:].broadcast_to([P, MH, half])
                    t1, t2 = (rtmp[:, i, :].rearrange("p (h c) -> p h c", h=MH) for i in range(2))
                    rotate(q_[:, :, NOPE:NOPE + half], q_[:, :, NOPE + half:], cos, sin, t1, t2).then_inc(uq_done, 1)
                elif kind == "kn":
                    wait_filled(dve, job)
                    v.tensor_copy(mlaK[0:NOPE, job[1], :], ps(job)[0:NOPE, :]).then_inc(done, 1)
                elif kind == "wukT":
                    wait_filled(dve, job)
                    v.tensor_copy(wukT[0:NOPE, 4 * job[1]:4 * job[1] + 4, :],
                                  ps(job)[0:NOPE, :].rearrange("p (k n) -> p k n", k=4)).then_inc(done, 1)
                elif kind in ("dq", "dk"):
                    t, n = job[1], rot_no[job] - 1
                    wait_drained(dve, job)
                    if n:
                        dve.wait_ge(rot_done, n)
                    else:
                        dve.wait_ge(uq_done, TILES)
                    q_ = rot[:, n % 2, :].rearrange("p (h c) -> p h c", h=2 * DH)
                    half = DROT // 2
                    cos = roped[:, t:t + 1, 0:half].broadcast_to([P, 2 * DH, half])
                    sin = roped[:, t:t + 1, half:].broadcast_to([P, 2 * DH, half])
                    t1, t2 = (rtmp[:, i, 0:2 * DH * half].rearrange("p (h c) -> p h c", h=2 * DH) for i in range(2))
                    rotate(q_[:, :, 0:half], q_[:, :, half:DROT], cos, sin, t1, t2).then_inc(rot_done, 1)
                elif kind == "dkT":
                    wait_filled(dve, job)
                    v.tensor_copy(diffT[:, 1, :, tok(job[1])], ps(job)[:, :].rearrange("p (k n) -> p k n", k=4)).then_inc(done, 1)
                elif kind == "cacheT" and job[1] == "MS":
                    b = job[2]
                    wait_filled(dve, job)
                    dve.wait_ge(stored_ckv, 16 * 4)
                    v.tensor_copy(ckv_cT[:, b % 2, :], ps(job)[:, 0:PAST])
                    v.tensor_copy(kr_cT[NOPE:QK, b % 2, :], ps(job)[NOPE:QK, PAST:]).then_inc(done, 1)
                elif kind == "cacheT" and job[1] == "BS" and job[4] == 1:
                    wait_filled(dve, job)
                    v.tensor_copy(k_cT[:, (2 * job[3] + 1) % 4, :, :].rearrange("p a b -> p (a b)"), ps(job)[:, :]).then_inc(done, 1)
                elif kind in ("score", "score2") and ("score", job[1]) in exp_no:
                    s = job[1]
                    st = stats if kind == "score" else stats2
                    r = nth[s] % 8
                    wait_filled(dve, job)
                    v.tensor_reduce(st[:, 0, r:r + 1], ps(job)[:, 0:width(s)], AX_X, ALU.max, negate=True).then_inc(max_done, 1)
                elif kind == "score":
                    s = job[1]
                    n = width(s)
                    z = ps(job)[:, 0:n]
                    e = soft[:, nth[s] % 2, 0:n]
                    dve.wait_ge(soft_done, stick_no[s])
                    link(v.scalar_tensor_tensor(out=e, in0=z, scalar=0.0, in1=e, op0=ALU.max, op1=ALU.add))
                    link(v.tensor_tensor_scan(cum[:, 0:n][:, ::-1], ones[:, 0:n], e[:, ::-1], 0.0, ALU.mult, ALU.add))
                    v.tensor_tensor(probs[:, nth[s] % 3, 0:n], z, cum[:, 0:n], ALU.subtract).then_inc(done, 1)
                elif kind == "weigh" and job[1] in weigh_no:
                    s = job[1]
                    n, r = width(s), nth[s] % 8
                    p = probs[:, nth[s] % 3, 0:n]
                    wait_drained(dve, ("score", s))
                    if s[0] == "D":
                        wait_drained(dve, ("score2", s))
                    link(v.reciprocal(coef[:, 0, r:r + 1], stats[:, 1, r:r + 1]))
                    if s[0] == "MS":
                        v.tensor_scalar(p, p, coef[:, 0, r:r + 1], None, ALU.mult).then_inc(weigh_done, 1)
                    elif s[0] == "D":
                        p2 = probs2[:, nth[s] % 2, 0:n]
                        link(v.reciprocal(coef[:, 1, r:r + 1], stats2[:, 1, r:r + 1]))
                        link(v.tensor_scalar(p2, p2, coef[:, 1, r:r + 1], lam[:, 5:6], ALU.mult, ALU.mult))
                        v.scalar_tensor_tensor(out=p, in0=p, scalar=coef[:, 0, r:r + 1], in1=p2,
                                               op0=ALU.mult, op1=ALU.add).then_inc(weigh_done, 1)
                    else:
                        v.tensor_scalar(csel[:, s[1] % 2, :], sel[:, :], coef[:, 0, r:r + 1], sign[:, 0:1],
                                        ALU.mult, ALU.mult).then_inc(weigh_done, 1)
                elif kind == "turn":
                    s = job[1]
                    w = wT[:, nth[s] % 2, :]
                    m = DIFF_ROWS if s[0] == "DS" else P
                    wait_filled(dve, job)
                    if s[0] in ("M", "D", "B"):
                        v.tensor_copy(w[:, 0:width(s)], ps(job)[:, 0:width(s)]).then_inc(done, 1)
                    else:
                        v.tensor_copy(w[:, 0:2 * m], ps(job)[:, 0:2 * m])
                        v.tensor_copy(w[0:NEW, 2 * m:3 * m], ps(job)[0:NEW, 2 * m:3 * m]).then_inc(done, 1)
                elif kind == "value" and job[1][0] == "M":
                    s = job[1]
                    _, t, h = s
                    r = nth[s] % 8
                    wait_filled(dve, job)
                    wait_drained(dve, ("G", t))
                    wait_drained(dve, ("score", s))
                    link(v.reciprocal(coef[:, 0, r:r + 1], stats[:, 1, r:r + 1]))
                    g_ = gates[:, t, h * MV:(h + 1) * MV]
                    v.scalar_tensor_tensor(out=g_, in0=ps(job)[:, 0:MV], scalar=coef[:, 0, r:r + 1], in1=g_,
                                           op0=ALU.mult, op1=ALU.mult).then_inc(done, 1)
                elif kind == "value" and job[1][0] == "B":
                    _, g, t, h = job[1]
                    wait_filled(dve, job)
                    g_ = g1[:, g % 2, t, h * HD:(h + 1) * HD]
                    v.tensor_tensor(g_, ps(job)[:, 0:HD], g_, ALU.mult).then_inc(done, 1)
                elif kind == "value" and job[1][0] == "BS":
                    _, g, pair = job[1]
                    wait_filled(dve, job)
                    o = ps(job)[:, 0:P].rearrange("p (i k q) -> p k i q", i=2, k=2)
                    for par in range(2):
                        r = slice(HD * par, HD * (par + 1))
                        i = v.tensor_tensor(
                            oT[r, 2 * g:2 * g + 2, SEQ + 2 * pair * NEW:SEQ + 2 * (pair + 1) * NEW].rearrange("p k (i q) -> p k i q", i=2),
                            o[r, :, :, par * NEW:(par + 1) * NEW],
                            gsT[r, g % 2, :, 2 * pair * NEW:2 * (pair + 1) * NEW].rearrange("p k (i q) -> p k i q", i=2), ALU.mult)
                    i.then_inc(done, 1)
                elif kind == "om":
                    wait_filled(dve, job)
                    g_ = gates[:, S_TILE, 0:MLA_W]
                    v.tensor_tensor(g_, ps(job)[:, :], g_, ALU.mult).then_inc(done, 1)
                elif kind == "qblocks":
                    wait_drained(dve, ("dqT", S_TILE))
                    link(v.memset(qblk[:, :, :, :], 0.0))
                    for h in range(DH):
                        for i in range(2):
                            r = slice(HD * i, HD * (i + 1))
                            ins = v.tensor_copy(qblk[r, :, h, i * NEW:(i + 1) * NEW],
                                                diffT[r, 0, h, tok(S_TILE)].rearrange("p (b q) -> p b q", b=STREAMS))
                    ins.then_inc(blocks_done, 1)
                elif kind == "post":
                    t = job[1]
                    o = rot[:, t % 2, :]
                    if t < PT_TILES:
                        wait_drained(dve, ("value", ("D", t, DH - 1)))
                    else:
                        wait_drained(dve, ("od",))
                    o3 = o.rearrange("p (h c) -> p h c", h=DH)
                    s3 = sq2.rearrange("p (h c) -> p h c", h=DH)
                    link(v.tensor_tensor(sq2, o, o, ALU.mult))
                    link(v.tensor_reduce(ss[:, 0, 0:DH], s3, AX_X, ALU.add))
                    v.tensor_scalar(ss[:, 1, 0:DH], ss[:, 0, 0:DH], 1.0 / (2 * HD), EPS, ALU.mult, ALU.add).then_inc(pow_in, 1)
                    g_ = gates[:, t, MLA_W:].rearrange("p (h c) -> p h c", h=DH)
                    wait_drained(dve, ("gd", t))
                    link(v.tensor_tensor(g_, g_, g_sub[:, :].unsqueeze(1).broadcast_to([P, DH, 2 * HD]), ALU.mult))
                    dve.wait_ge(pow_out, pow_no[job])
                    link(v.tensor_tensor(o3, o3, ss[:, 2, 0:DH].unsqueeze(2).broadcast_to([P, DH, 2 * HD]), ALU.mult))
                    v.tensor_tensor(g_, g_, o3, ALU.mult).then_inc(post_done, 1)
                elif kind in ("outp", "out"):
                    _, layer, t, h = job
                    x_ = x_sb[:, t, h * 512:(h + 1) * 512]
                    if kind == "outp":
                        if layer == 0:
                            dve.wait_ge(xres_in, 16 * TILES)
                        wait_filled(dve, job)
                        v.scalar_tensor_tensor(out=x_, in0=x_, scalar=ALPHA, in1=ps(job)[:, :], op0=ALU.mult,
                                               op1=ALU.add).then_inc(done, 1)
                    else:
                        wait_drained(dve, ("outp", layer, t, h))
                        wait_filled(dve, job)
                        v.tensor_tensor(x_, x_, ps(job)[:, :], ALU.add).then_inc(done, 1)
                elif kind == "ln":
                    _, layer, t = job
                    gg = gains if layer == 0 else gains1
                    x_ = x_sb[:, t, :]
                    dve.wait_ge(gains_in if layer == 0 else gains1_in, 32)
                    for h in range(2):
                        wait_drained(dve, ("out", layer, t, h))
                    v.bn_stats(bn[:, 0, :], x_[:, 0:512])
                    link(v.bn_stats(bn[:, 1, :], x_[:, 512:]))
                    link(v.bn_aggr(mv[:, :], bn[:, :, :]))
                    v.tensor_scalar(mv[:, 1:2], mv[:, 1:2], EPS, None, ALU.add).then_inc(pow_in, 1)
                    dve.wait_ge(pow_out, pow_no[job])
                    link(v.tensor_scalar(x_, x_, mv[:, 0:1], rstd[:, 0:1], ALU.subtract, ALU.mult))
                    link(v.tensor_tensor(x_, x_, gg[:, 0, :], ALU.mult))
                    v.tensor_tensor(x_, x_, gg[:, 1, :], ALU.add).then_inc(ln_done, 1)
                elif kind == "kT":
                    _, g, t = job
                    if g == 0 and t == 0:
                        v.memset(ones[:, :], 1.0)
                        link(v.memset(qblk1[:, :, :, :, :], 0.0))
                    wait_filled(dve, job)
                    v.tensor_copy(kT[:, g % 2, :, tok(t)], ps(job)[:, 0:2 * P].rearrange("p (k n) -> p k n", k=2)).then_inc(done, 1)
                elif kind == "gblocks":
                    g = job[1]
                    wait_drained(dve, ("qs", g))
                    for h in range(GH):
                        r = slice(HD * (h % 2), HD * (h % 2) + HD)
                        ins = v.tensor_copy(qblk1[r, g % 2, :, h // 2, h * NEW:(h + 1) * NEW],
                                            qT1[r, g % 2, h // 2, tok(S_TILE)].rearrange("p (b q) -> p b q", b=STREAMS))
                    ins.then_inc(blocks_done, 1)
                elif kind in ("g", "gs"):
                    g = job[1]
                    e = gtmp[:, gate_no[job] % 2, 0:GW]
                    dve.wait_ge(gate_e, gate_no[job])
                    link(v.tensor_scalar(e, e, 1.0, None, ALU.add))
                    link(v.reciprocal(e, e))
                    dst = g1[:, g % 2, job[2], :] if kind == "g" else gsT[:, g % 2, :, :].rearrange("p a b -> p (a b)")
                    v.tensor_tensor(dst, ps(job)[:, 0:GW], e, ALU.mult).then_inc(done, 1)
                elif kind == "oT":
                    _, g, t = job
                    wait_filled(dve, job)
                    v.tensor_copy(oT[:, 2 * g:2 * g + 2, tok(t)], ps(job)[:, 0:2 * P].rearrange("p (k n) -> p k n", k=2)).then_inc(done, 1)


_INS = ['x_prompt', 'x_sample', 'cache_mla_ckv', 'cache_mla_krope', 'cache_diff_k', 'cache_diff_v', 'cache_sb_k',
        'cache_sb_v', 'w_in_even', 'q_norm_g', 'w_uq', 'kv_norm_g', 'w_uk', 'w_uv', 'diff_lambda_q',
        'diff_lambda_k', 'diff_subln_g', 'w_out_even', 'ln_even_g', 'ln_even_b', 'w_in_odd', 'w_out_odd',
        'ln_odd_g', 'ln_odd_b']
_OUTS = [(1, SEQ, D), (STREAMS, NEW, D), (1, 1, SEQ, KVL), (1, 1, SEQ, ROT), (1, 1, SEQ, DH, 2, HD),
         (1, 1, SEQ, DH, 2 * HD), (1, 1, SEQ, 16, HD), (1, 1, SEQ, 16, HD), (1, STREAMS, NEW, KVL),
         (1, STREAMS, NEW, ROT), (1, STREAMS, NEW, DH, 2, HD), (1, STREAMS, NEW, DH, 2 * HD),
         (1, STREAMS, NEW, 16, HD), (1, STREAMS, NEW, 16, HD)]


def shape_constants():
    r = np.arange(P)
    neg = np.float32(-1e30)
    masks = np.zeros((P, MASKS), np.float32)
    masks[:, 0:P] = np.where(r[None, :] // 64 <= r[:, None] // 64, 0, neg)
    masks[:, P:2 * P] = np.where(r[None, :] < r[:, None], 0, neg)
    masks[:, 2 * P:] = np.where(r[None, :NEW] < r[:, None] % NEW, 0, neg)
    sel = (r[:, None] // (2 * NEW) * NEW + r[:, None] % NEW == np.arange(DIFF_ROWS)[None, :]).astype(np.float32)
    second = r // NEW % 2
    sign = np.stack([1 - second, second], 1).astype(np.float32)
    pos = np.concatenate([np.arange(SEQ), PAST + r % NEW]).astype(np.float32)

    def rope(rot, theta):
        half = rot // 2
        inv = np.exp(np.float32(-math.log(theta)) * np.arange(half, dtype=np.float32) * np.float32(2.0 / rot))
        ang = pos[:, None] * inv[None, :].astype(np.float32)
        both = np.concatenate([np.cos(ang), np.sin(ang)], 1).astype(np.float32)
        return np.ascontiguousarray(both.reshape(TILES, P, rot).transpose(1, 0, 2))

    return {"c_ident": np.eye(P, dtype=np.float32), "c_masks": masks, "c_sel": sel, "c_sign": sign,
            "c_ropem": rope(ROT, 10000.0), "c_roped": rope(DROT, 500000.0)}


def kernel(**inputs):
    import concourse.bacc as _bacc
    from concourse.bass_utils import run_bass_kernel_spmd as _run

    nc = _bacc.Bacc("TRN2", target_bir_lowering=False, num_devices=1)
    arrays, aps = {}, {}
    for name, x in list((n, inputs[n]) for n in _INS) + list(shape_constants().items()):
        x = np.ascontiguousarray(x)
        arrays[f"in_{name}_dram"] = x
        aps[name] = nc.dram_tensor(f"in_{name}_dram", x.shape, mybir.dt.from_np(x.dtype), kind="ExternalInput").ap()
    outs = [nc.dram_tensor(f"out_{i}_dram", shape, F32, kind="ExternalOutput").ap() for i, shape in enumerate(_OUTS)]
    trunk_kernel(nc, aps, outs)
    r = _run(nc, [arrays], core_ids=[0])
    return tuple(r.results[0][f"out_{i}_dram"] for i in range(len(_OUTS)))
```

```python
from contextlib import ExitStack
import math

import numpy as np

import concourse.bass as bass
from concourse import mybir

F32 = mybir.dt.float32
BF16 = mybir.dt.bfloat16
ALU = mybir.AluOpType
ACT = mybir.ActivationFunctionType
AX_X = mybir.AxisListType.X

P = 128
D = 1024
KD = D // P
SEQ, STREAMS, NEW, PAST = 512, 8, 16, 256
PT_TILES = SEQ // P
TILES = PT_TILES + 1
S_TILE = PT_TILES
TOK = TILES * P
CKV_SLOTS = 2
STAGES = 3
F32R = mybir.dt.float32r
MASKS = 2 * P + NEW
SMALL = 13
ALPHA = 4 ** 0.25
EPS = 1e-5
MH, NOPE, ROT, MV = 8, 64, 32, 64
QK = NOPE + ROT
QL, KVL = 256, 128
SEC_A = QL + KVL + ROT
DH, HD, DROT = 4, 64, 16
MLA_W = MH * MV
DIFF_W = DH * 2 * HD
LAM_INIT = 0.8 - 0.6 * math.exp(-0.3 * 0)
MLA_SCALE = QK ** -0.5
HEAD_SCALE = HD ** -0.5
GROUPS, GH = 4, 4
GW = GH * HD
DIFF_ROWS = DH * NEW



def pipeline(steps, fillers, place, after=None, ahead=None):
    jobs, done, later = [], 0, {}
    turns = len(steps) + 3

    def between(i, here):
        nonlocal done
        if place != here:
            return []
        want = len(fillers) * (i + 1) // turns
        out = [job for bundle in fillers[done:want] for job in bundle]
        done = want
        return later.pop(i, []) + out if place == "end" else out + later.pop(i, [])

    for job in (ahead(steps[0]) if ahead else []):
        jobs.append(job)
    for i in range(turns):
        if i < len(steps):
            jobs.append(("score", steps[i]))
            if steps[i][0] == "D":
                jobs.append(("score2", steps[i]))
            if ahead and i + 1 < len(steps):
                jobs += ahead(steps[i + 1])
        if 1 <= i <= len(steps):
            jobs.append(("weigh", steps[i - 1]))
        jobs += between(i, "turn")
        if 2 <= i < len(steps) + 2:
            jobs.append(("turn", steps[i - 2]))
        jobs += between(i, "value")
        if 3 <= i:
            jobs.append(("value", steps[i - 3]))
            for turns_on, job in (after(steps[i - 3]) if after else []):
                later.setdefault(i + turns_on, []).append(job)
        jobs += between(i, "end")
    for i in sorted(later):
        jobs += later[i]
    return jobs


def mingle(prompt, samples):
    n = len(prompt) // len(samples)
    return [s for i, one in enumerate(samples) for s in prompt[i * n:(i + 1) * n] + [one]]


HALF = 256
QUARTERS = 4
SECTIONS = [name + i for name in ("A", "G", "dk", "dv", "dq", "gd", "out00", "out01") for i in "01"]
for _g in range(GROUPS):
    SECTIONS += [f"k{_g}", f"v{_g}", f"q{_g}", f"g{_g}"]
SECTIONS += ["out100", "out101", "out110", "out111"]


def convert(*sections):
    return [("cvt", QUARTERS * SECTIONS.index(s) + k) for s in sections for k in range(QUARTERS)]


def beside(bundles, conversions):
    n = len(bundles)
    return [b + conversions[len(conversions) * i // n:len(conversions) * (i + 1) // n] for i, b in enumerate(bundles)]


def flat_jobs(bundles):
    return [job for bundle in bundles for job in bundle]


COMPLETE = (0, 1, 2)


def out_blocks(job):
    _, layer, part, t, _ = job
    if part == 0:
        return range(0, 4)
    if layer == 0 or t in COMPLETE:
        return range(4, 8)
    return range(4, 6) if part == 1 else range(6, 8)


def last_part(layer, t):
    return 1 if layer == 0 or t in COMPLETE else 2


def make_schedule():
    tiles = range(TILES)
    jobs = [("xT", 0, t, h) for t in tiles for h in range(2)] + convert("A0", "A1")
    jobs += [("A", t, 0) for t in tiles]
    jobs += flat_jobs(beside([[("A", t, 1)] for t in tiles], convert("G0"))) + convert("G1") + [("rms",)]
    jobs += [("G", t, 0) for t in tiles]
    jobs += flat_jobs(beside([[("G", t, 1)] for t in tiles], convert("dk0")))
    jobs += [("latT", t) for t in tiles] + [("lam",)]
    for t in tiles:
        jobs += [("uq", t, 0), ("uq", t, 1), ("uqrope", t)]
        if t:
            jobs += [("qT", t - 1, 0), ("qT", t - 1, 1)]
    jobs += [("kn", h) for h in range(MH)] + [("wukT", 0), ("wukT", 1)]
    jobs += [("qT", S_TILE, 0), ("qT", S_TILE, 1)]
    jobs += flat_jobs(beside([[("vm", t)] for t in range(PT_TILES)], convert("dk1")))
    jobs += [("qa", 0), ("qa", 1)]

    fill = [[("clear",), ("dk", 0)]]
    for t in tiles[1:]:
        fill.append([("dk", t), ("dkT", t - 1)])
    fill += [[("dkT", S_TILE)] + convert("dv0")[:2], convert("dv0")[2:]]
    fill += beside([[("dv", t, 0)] for t in tiles], convert("dv1"))
    fill += beside([[("dv", t, 1)] for t in tiles], convert("dq0"))
    fill += [convert("dq1")[:2], convert("dq1")[2:], [("dq", S_TILE)], [("dq", 0)]]
    steps = mingle([("M", t, h) for t in range(PT_TILES) for h in range(MH)], [("MS", b) for b in range(STREAMS)])
    jobs += pipeline(steps, fill, "end", ahead=lambda s: [("cacheT",) + s] if s[0] == "MS" else [])
    jobs += [("dqT", S_TILE), ("dqT", 0), ("om",), ("qblocks",)]

    fill = []
    for t in range(1, PT_TILES):
        fill += [[("dq", t)], [("dqT", t)]]
    fill += [convert("gd0")[:2], convert("gd0")[2:], convert("gd1")[:2], convert("gd1")[2:]]
    fill += [[("gd", 0), ("gate", 0)], [("gd", 1), ("gate", 1)], [("gd", 2)], [], [("gate", 2), ("gd", 3)], []]
    steps = mingle([("D", t, h) for t in range(PT_TILES) for h in range(DH)], [("DS", b) for b in range(STREAMS)])
    jobs += pipeline(
        steps, fill, "end",
        ahead=lambda s: [("cacheT",) + s + (k,) for k in range(2)] if s[0] == "DS" else [],
        after=lambda s: [(1, ("post", s[1]))] if s[0] == "D" and s[2] == DH - 1 else [])
    jobs += [("gd", S_TILE), ("gate", 3), ("od",)]
    jobs += flat_jobs(beside([[("ogT", t, 0)] for t in tiles], convert("out000")))
    jobs += [("out", 0, 0, 0, 0)]
    jobs += flat_jobs(beside([[("ogT", 0, 1)], [("ogT", 1, 1), ("out", 0, 0, 1, 0)], [("ogT", 2, 1)]], convert("out001")))
    jobs += [("post", S_TILE), ("gate", S_TILE), ("out", 0, 0, 0, 1), ("ogT", 3, 1), ("out", 0, 0, 1, 1), ("ogT", S_TILE, 1)]
    jobs += [("out", 0, 0, t, 0) for t in tiles[2:]]
    jobs += flat_jobs(beside([[("out", 0, 0, t, 1)] for t in tiles[2:]], convert("out010")))
    jobs += flat_jobs(beside([[("out", 0, 1, t, 0)] for t in tiles[:2]], convert("out011")))
    for t in tiles:
        if t > 1:
            jobs += [("out", 0, 1, t, 0)]
        if t == S_TILE:
            jobs += convert("k0")
        jobs += [("out", 0, 1, t, 1), ("ln", 0, t)] + ([("shift", 0, t - 1)] if t else [])
        if t > 2:
            jobs += [("xT", 1, t - 3, 0), ("xT", 1, t - 3, 1)]
    jobs += [("shift", 0, S_TILE)]

    def project(g):
        if g:
            keys = [[("k", g, 0)]] + [[("k", g, t), ("kT", g, t - 1)] for t in tiles[1:]]
        else:
            keys = [[("k", g, 0), ("xT", 1, 2, 0), ("xT", 1, 2, 1)], [("k", g, 1), ("kT", g, 0), ("xT", 1, 3, 0), ("xT", 1, 3, 1)],
                    [("k", g, 2), ("kT", g, 1)], [("k", g, 3), ("kT", g, 2)]]
        fill = beside(keys, convert(f"v{g}"))
        values = [[("v", g, t)] for t in tiles]
        if g:
            values[0] += [("kT", g, S_TILE)]
            fill += beside(values, convert(f"q{g}"))
        else:
            fill += values[:2] + [[("kT", g, 3), ("xT", 1, S_TILE, 0), ("xT", 1, S_TILE, 1), ("k", g, S_TILE)]]
            values[2] += [("kT", g, S_TILE)]
            fill += beside(values[2:], convert(f"q{g}"))
        fill += beside([[("q", g, blk, part)] for blk in range(2) for part in range(2)], convert(f"g{g}"))
        return fill + beside([[("g", g, S_TILE)], [("g", g, 0), ("gsT", g)]] + [[("g", g, t)] for t in tiles[1:PT_TILES]],
                             convert(f"k{g + 1}" if g + 1 < GROUPS else "out100"))

    jobs += flat_jobs(project(0))
    for g in range(GROUPS):
        jobs += [("gblocks", g)]
        steps = mingle([("B", g, t, h) for t in range(PT_TILES) for h in range(GH)],
                       [("BS", g, p) for p in range(STREAMS // 2)])
        if g + 1 < GROUPS:
            fill = project(g + 1)
        else:
            fill = [[("ocvt", 0), ("ocvt", 1)], [("ocvt", 2), ("ocvt", 3)]]
            fill += beside([[("out", 1, 0, t, 0)] for t in tiles], convert("out101"))
            fill += beside([[("out", 1, 0, t, 1)] for t in tiles], convert("out110") + [("ocvt", 4), ("ocvt", 5)])
            fill += beside([[("out", 1, 1, t, 0)] for t in (0, 1)], convert("out111"))
            fill += [[("out", 1, 1, 0, 1), ("ln", 1, 0)], [("shift", 1, 0), ("out", 1, 1, 1, 1), ("ln", 1, 1)]]
            fill += [[("shift", 1, 1), ("out", 1, 1, 2, 0)], [("out", 1, 1, 2, 1), ("ln", 1, 2)]]
            fill += [[("shift", 1, 2), ("out", 1, 1, 3, 0), ("out", 1, 1, 3, 1)], [("out", 1, 1, S_TILE, 0), ("out", 1, 1, S_TILE, 1)]]
        jobs += pipeline(
            steps, fill, "value",
            ahead=lambda s: [("cacheT",) + s + (k,) for k in range(2)] if s[0] == "BS" else [],
            after=lambda s: [(1, ("oT", s[1], s[2]))] if s[0] == "B" and s[3] == GH - 1 else [])
    jobs += [("ocvt", "samples")]
    for t in (3, S_TILE):
        jobs += [("out", 1, 2, t, 0), ("out", 1, 2, t, 1), ("ln", 1, t)]
    jobs += [("shift", 1, 3), ("shift", 1, S_TILE)]
    return jobs


BANKS = {"proj": 2, "score": 2, "turn": 3, "value": 1}
RING_OF = {}
for _k in ("A", "G", "uq", "kn", "vm", "qa", "dq", "dk", "dv", "gd", "om", "out", "k", "v", "q", "g"):
    RING_OF[_k] = "proj"
for _k in ("xT", "latT", "qT", "wukT", "dqT", "dkT", "cacheT", "turn", "ogT", "od", "kT", "oT", "gsT"):
    RING_OF[_k] = "turn"
for _k in ("score", "score2"):
    RING_OF[_k] = "score"
RING_OF["value"] = "value"


def sections_of(job):
    kind = job[0]
    if kind in ("A", "G", "dv"):
        return [f"{kind}{job[2]}"]
    if kind in ("dk", "dq", "gd"):
        return [kind + "0", kind + "1"]
    if kind in ("k", "v", "q", "g"):
        return [f"{kind}{job[1]}"]
    if kind == "out":
        return [f"out{job[1]}{min(job[2], 1)}{job[4]}"]
    return []


def assign_banks(schedule):
    uses = {r: 0 for r in BANKS}
    where = {}
    for job in schedule:
        ring = RING_OF.get(job[0])
        if ring:
            n = uses[ring]
            where[job] = (f"{ring}{n % BANKS[ring]}", n // BANKS[ring] + 1)
            uses[ring] = n + 1
    return where


def turn_blocks(step):
    if step[0] in ("M", "D"):
        return [(j * P, P) for j in range(step[1] + 1)]
    if step[0] == "B":
        return [(j * P, P) for j in range(step[2] + 1)]
    return [(0, P), (P, P), (PAST, NEW)]


def width(step):
    a, n = turn_blocks(step)[-1]
    return a + n




def trunk_kernel(nc, a, out):
    schedule = make_schedule()
    where = assign_banks(schedule)
    steps = [j[1] for j in schedule if j[0] == "score"]
    nth = {s: i for i, s in enumerate(steps)}
    exp_steps = [s for s in steps if s[0] in ("M", "MS", "D", "DS")]
    sb_steps = [s for s in steps if s[0] in ("B", "BS")]

    ctx = ExitStack()

    def sem(name):
        return ctx.enter_context(nc.semaphore(name))

    def alloc(stack, name, shape, dt=F32):
        return stack.enter_context(nc.sbuf_tensor(name, [P] + shape, dt))

    with ctx:
        def sb(name, shape, dt=F32):
            return alloc(ctx, name, shape, dt)

        x_sb = sb("x_sb", [TILES, D])
        xT_hi = sb("xT_hi", [KD, TOK], F32R)
        xT_lo = sb("xT_lo", [KD, TOK], F32R)
        w_hi = sb("w_hi", [2, KD * HALF], F32R)
        w_lo = sb("w_lo", [2, KD * HALF], F32R)
        stage = sb("stage", [STAGES, 512])
        probs = sb("probs", [3, 512])
        work8 = sb("work8", [4, 512])
        probs2 = work8[:, 0:2, :]
        wT = work8[:, 2:4, :]
        latT = work8[:, :, :].rearrange("p a b -> p (a b)")[:, 0:3 * TOK].rearrange("p (a b) -> p a b", a=3)
        ident = sb("ident", [P])
        identb = sb("identb", [P], BF16)
        mask_chunk = sb("mask_chunk", [P], BF16)
        mask_causal = sb("mask_causal", [P], BF16)
        mask_new = sb("mask_new", [NEW], BF16)
        stats = sb("stats", [2, 8])
        stats2 = sb("stats2", [2, 8])
        coef = sb("coef", [2, 8])
        bn = sb("bn", [2, 6])
        mv = sb("mv", [2, 2])
        rstd = sb("rstd", [2, 1])
        minus_half = sb("minus_half", [10])

        l0 = ExitStack()
        lat = alloc(l0, "lat", [TILES, SEC_A])
        gates = alloc(l0, "gates", [TILES, MLA_W])
        dv = alloc(l0, "dv", [TILES, DIFF_W])
        dkT = alloc(l0, "dkT", [DH, TOK])
        mlaK = alloc(l0, "mlaK", [MH, SEQ])
        vm = alloc(l0, "vm", [PT_TILES, MLA_W])
        uq = alloc(l0, "uq", [2, MH * QK])
        ckvTs = alloc(l0, "ckvTs", [P])
        krTs = alloc(l0, "krTs", [P])
        ckv_c = alloc(l0, "ckv_c", [CKV_SLOTS, 2, KVL])
        kr_c = alloc(l0, "kr_c", [(2 + 2 * STREAMS) * ROT])
        w_uq = alloc(l0, "w_uq", [2, MH * QK])
        w_uk = alloc(l0, "w_uk", [MH * NOPE])
        w_uv = alloc(l0, "w_uv", [MLA_W])
        g_q = alloc(l0, "g_q", [QL])
        g_kv = alloc(l0, "g_kv", [KVL])
        g_sub = alloc(l0, "g_sub", [2 * HD])
        lam = alloc(l0, "lam", [8])
        ropem = alloc(l0, "ropem", [TILES, ROT])
        roped = alloc(l0, "roped", [TILES, DROT])
        rtmp = alloc(l0, "rtmp", [2, P])
        newv = alloc(l0, "newv", [512])
        newckv = alloc(l0, "newckv", [2, KVL])
        sel = alloc(l0, "sel", [DIFF_ROWS])
        sign = alloc(l0, "sign", [2])
        csel = alloc(l0, "csel", [2, DIFF_ROWS])
        ss = alloc(l0, "ss", [3, 10])
        qT = x_sb[:, :, :].rearrange("p a b -> p (a b)").rearrange("p (h n) -> p h n", h=MH)
        flat = lambda b: b[:, :, :].rearrange("p a b -> p (a b)")
        lam4 = flat(rtmp).rearrange("p (a b) -> p a b", a=4)
        rot = flat(uq)[:, 0:1024].rearrange("p (a b) -> p a b", a=2)
        sq2 = flat(uq)[:, 1024:1536]
        qa = flat(work8)[:, 0:1024].rearrange("p (b n) -> p b n", b=STREAMS)
        wukT = flat(probs)[:, 512:1536].rearrange("p (h n) -> p h n", h=MH)
        o_mlaT = flat(lat)[:, 0:1024].rearrange("p (h n) -> p h n", h=MH)
        ckv_cT = flat(lat)[:, 1024:1536].rearrange("p (a b) -> p a b", a=2)
        kr_cT = flat(lat)[:, 1536:2048].rearrange("p (a b) -> p a b", a=2)
        dqT = flat(x_sb)[:, 0:DH * TOK].rearrange("p (h n) -> p h n", h=DH)
        od_n = flat(x_sb)[:, DH * TOK:].rearrange("p (t n) -> p t n", t=TILES)
        qblk = flat(w_uq)[:, 0:1024].rearrange("p (b h n) -> p b h n", b=STREAMS, h=DH)
        od_T = flat(w_uq)[:, 1024:1536].rearrange("p (h n) -> p h n", h=DH)
        lat_flat = lat[:, :, :].rearrange("p a b -> p (a b)")
        gains = [lat_flat[:, 0:D], lat_flat[:, D:2 * D]]
        caches = mlaK[:, :, :].rearrange("p a b -> p (a b)").rearrange("p (r c b n) -> p r c b n", r=2, c=2, b=2)
        dk_c, dv_c = caches[:, 0], caches[:, 1]
        dk_cT = vm[:, :, :].rearrange("p a b -> p (a b)").rearrange("p (s h k) -> p s h k", s=2, h=DH)
        sq = flat(dkT)
        l0.close()

        l1 = ExitStack()
        v_n = alloc(l1, "v_n", [2, TILES, GW])
        k_n = alloc(l1, "k_n", [2, GW])
        kT = alloc(l1, "kT", [2, 2, TOK])
        qT1 = alloc(l1, "qT1", [2, 2, TOK])
        g1 = alloc(l1, "g1", [2, PT_TILES, GW])
        gsT = alloc(l1, "gsT", [2, 2, P])
        gtmp = alloc(l1, "gtmp", [2, GW])
        oT = alloc(l1, "oT", [KD, TOK])
        qblk1 = alloc(l1, "qblk1", [STREAMS, 2, GH * NEW])
        k_c = alloc(l1, "k_c", [2, 2, GW])
        v_c = alloc(l1, "v_c", [2, 2, GW])
        newv1 = alloc(l1, "newv1", [2, GW])
        k_cT = alloc(l1, "k_cT", [2, 2, PAST])
        soft = alloc(l1, "soft", [2, 512])
        cum = alloc(l1, "cum", [512])
        gains1 = [kT[:, 0, :, :].rearrange("p a b -> p (a b)")[:, 0:D], v_n[:, 0, :, :].rearrange("p a b -> p (a b)")[:, 0:D]]
        l1.close()

        bank = {f"{r}{i}": ctx.enter_context(nc.psum_tensor(f"{r}{i}", [P, 512], F32))
                for r in BANKS for i in range(BANKS[r])}
        filled = {b: sem(f"filled_{b}") for b in bank}
        drained = {b: sem(f"drained_{b}") for b in bank}
        consts_in, small_in = sem("consts_in"), sem("small_in")
        xres_in = [sem(f"xres_in{t}") for t in range(TILES)]
        x_in = [sem(f"x_in{t}") for t in range(TILES)]
        gains_in, gains1_in = sem("gains_in"), sem("gains1_in")
        stage_in = [sem(f"stage_in{i}") for i in range(STAGES)]
        hi_done, cvt_done = sem("hi_done"), sem("cvt_done")
        xhi_done = sem("xhi_done")
        ocvt_hi, ocvt_done = sem("ocvt_hi"), sem("ocvt_done")
        ckv_in = [sem(f"ckv_in{i}") for i in range(CKV_SLOTS)]
        kr_in, newv_in = sem("kr_in"), sem("newv_in")
        newckv_in = [sem(f"newckv_in{i}") for i in range(2)]
        dk_in = [sem(f"dk_in{i}") for i in range(2)]
        dv_in = [sem(f"dv_in{i}") for i in range(2)]
        kc_in = [sem(f"kc_in{i}") for i in range(2)]
        vc_in = [sem(f"vc_in{i}") for i in range(2)]
        rms_done, uq_done, rot_done = sem("rms_done"), sem("uq_done"), sem("rot_done")
        setup_done = sem("setup_done")
        blocks_done = sem("blocks_done")
        max_done, weigh_done = sem("max_done"), sem("weigh_done")
        soft_done, stick_done = sem("soft_done"), sem("stick_done")
        dve_lam, act_lam = sem("dve_lam"), sem("act_lam")
        gate_e = sem("gate_e")
        pow_in, pow_out = sem("pow_in"), sem("pow_out")
        post_done, ln_done = sem("post_done"), sem("ln_done")
        scale_done, norm_done, gained = sem("scale_done"), sem("norm_done"), sem("gained")
        dve_step, act_step, pool_step = sem("dve_step"), sem("act_step"), sem("pool_step")
        stored = sem("stored")
        stored_ckv, stored_dv = sem("stored_ckv"), sem("stored_dv")
        stored_v = [sem(f"stored_v{g}") for g in range(GROUPS)]
        stored_rot = [sem(f"stored_rot{i}") for i in range(2)]
        stored_kn = [sem(f"stored_kn{i}") for i in range(2)]
        stored_vn = [sem(f"stored_vn{i}") for i in range(2)]

        def ps(job):
            return bank[where[job][0]]

        def wait_filled(eng, job):
            eng.wait_ge(filled[where[job][0]], where[job][1])

        def wait_drained(eng, job):
            eng.wait_ge(drained[where[job][0]], where[job][1])

        def wait_bank(eng, job):
            b, n = where[job]
            if n > 1:
                eng.wait_ge(drained[b], n - 1)

        def tok(t):
            return slice(t * P, (t + 1) * P)

        def new(b):
            return slice(SEQ + b * NEW, SEQ + (b + 1) * NEW)

        def ordinal(kinds, pick=lambda j: True):
            js = [j for j in schedule if j[0] in kinds and pick(j)]
            return {j: i + 1 for i, j in enumerate(js)}

        pow_no = ordinal(("rms", "post", "ln"))
        rot_no = ordinal(("dq", "dk"))
        ln_no = ordinal(("ln",))
        gate_no = ordinal(("g",))
        two_parts_no = ordinal(("xT", "ogT", "oT"), lambda j: j[0] != "oT" or j[1] == GROUPS - 1)
        ocvt_no = ordinal(("ocvt",))
        kn_no = ordinal(("k",))
        blocks_no = ordinal(("qblocks", "gblocks"))
        exp_no = {s: i + 1 for i, s in enumerate(
            j for j in schedule if j[0] in ("score", "score2") and j[1][0] in ("M", "MS", "D", "DS"))}
        weigh_no = {s: i + 1 for i, s in enumerate(s for s in exp_steps if s[0] != "M")}
        units = {}
        for j in schedule:
            for sec in sections_of(j):
                units.setdefault(sec, [j, j])[1] = j
        stick_no = {s: i + 1 for i, s in enumerate(sb_steps)}

        w0 = a["w_in_even"].rearrange("a k c -> (a k) c")
        w1 = a["w_in_odd"].rearrange("a k c -> (a k) c")
        wo = [a["w_out_even"].rearrange("a k c -> (a k) c"), a["w_out_odd"].rearrange("a k c -> (a k) c")]
        x_p = a["x_prompt"].rearrange("b (t p) d -> p (b t) d", p=P)
        x_s = a["x_sample"].rearrange("b q d -> (b q) d")
        ckv_cache = a["cache_mla_ckv"].rearrange("a b (h p) c -> p (a b) h c", p=P)
        kr_cache = a["cache_mla_krope"].rearrange("a b (h p) c -> p (a b h) c", p=P)
        dk_cache = a["cache_diff_k"].rearrange("a b (h p) n i d -> p (a b) h (n i d)", p=P)
        dv_cache = a["cache_diff_v"].rearrange("a b (h p) n d -> p (a b) h (n d)", p=P)
        sk_cache = a["cache_sb_k"].rearrange("a b (h p) n d -> p (a b) h (n d)", p=P)
        sv_cache = a["cache_sb_v"].rearrange("a b (h p) n d -> p (a b) h (n d)", p=P)
        y_p = out[0].rearrange("b (t p) d -> t p (b d)", p=P)
        y_s = out[1].rearrange("b q d -> (b q) d")
        ckv_p = out[2].rearrange("a b (t p) c -> p (a b t) c", p=P)
        kr_p = out[3].rearrange("a b (t p) c -> p (a b t) c", p=P)
        dk_p = out[4].rearrange("a b (t p) n i d -> t p (a b n i d)", p=P)
        dv_p = out[5].rearrange("a b (t p) n d -> t p (a b n d)", p=P)
        sk_p = out[6].rearrange("a b (t p) n d -> t p (a b n d)", p=P)
        sv_p = out[7].rearrange("a b (t p) n d -> t p (a b n d)", p=P)
        ckv_s = out[8].rearrange("a b q c -> (a b q) c")
        kr_s = out[9].rearrange("a b q c -> (a b q) c")
        dk_s = out[10].rearrange("a b q n i d -> (a b q) (n i d)")
        dv_s = out[11].rearrange("a b q n d -> (a b q) (n d)")
        sk_s = out[12].rearrange("a b q n d -> (a b q) (n d)")
        sv_s = out[13].rearrange("a b q n d -> (a b q) (n d)")

        block = ctx.enter_context(nc.Block())

        @block.sync
        def _(sp):
            C_Q, C_G = SEC_A + MLA_W, SEC_A
            column0 = {"A": 0, "G": C_G, "dq": C_Q, "dk": C_Q + DIFF_W, "dv": C_Q + 2 * DIFF_W, "gd": C_Q + 3 * DIFF_W}

            def load_quarter(n):
                sec, k = SECTIONS[n // QUARTERS], n % QUARTERS
                dst, arrived = stage[:, n % STAGES, :], stage_in[n % STAGES]
                if sec[:3] == "out":
                    layer, part, half = int(sec[3]), int(sec[4]), int(sec[5])
                    row = (4 * part + k) * P
                    sp.dma_start(dst, wo[layer][row:row + P, half * 512:(half + 1) * 512]).then_inc(arrived, 16)
                    return
                if sec[:-1] in column0:
                    w, c0 = w0, column0[sec[:-1]] + HALF * int(sec[-1])
                else:
                    w, c0 = w1, "qkvg".index(sec[0]) * D + int(sec[1]) * GW
                n = SEC_A - HALF if sec == "A1" else HALF
                sp.dma_start(dst.rearrange("p (k c) -> p k c", k=2)[:, :, 0:n],
                             w[2 * k * P:(2 * k + 2) * P, c0:c0 + n].rearrange("(k p) c -> p k c", p=P)).then_inc(arrived, 16)

            for t in range(TILES):
                src = x_p[:, t, :] if t < PT_TILES else x_s
                sp.dma_start(x_sb[:, t, :], src).then_inc(x_in[t], 16)
                if t == 0:
                    sp.dma_start(ident[:, :], a["c_ident"]).then_inc(consts_in, 16)
                    for n in range(STAGES):
                        load_quarter(n)
            sp.dma_start(probs[:, 0, 0:MASKS], a["c_masks"]).then_inc(small_in, 16)
            for buf, name in ((sel, "c_sel"), (sign, "c_sign")):
                sp.dma_start(buf[:, :], a[name]).then_inc(small_in, 16)
            sp.dma_start(ropem[:, :, :], a["c_ropem"]).then_inc(small_in, 16)
            sp.dma_start(roped[:, :, :], a["c_roped"]).then_inc(small_in, 16)
            for buf, src in ((g_q, a["q_norm_g"]), (g_kv, a["kv_norm_g"]), (g_sub, a["diff_subln_g"])):
                sp.dma_start(buf[:, :], src.rearrange("a c -> (a c)").partition_broadcast(P)).then_inc(small_in, 16)
            sp.dma_start(lam4[:, 0:2, :], a["diff_lambda_q"].rearrange("a i d -> (a i) d").partition_broadcast(P)).then_inc(small_in, 16)
            sp.dma_start(lam4[:, 2:4, :], a["diff_lambda_k"].rearrange("a i d -> (a i) d").partition_broadcast(P)).then_inc(small_in, 16)
            sp.dma_start(w_uq[:, :, :], a["w_uq"].rearrange("a (k p) c -> p (a k) c", p=P)).then_inc(small_in, 16)
            sp.dma_start(w_uk[:, :], a["w_uk"].rearrange("a c h n -> (a c) (h n)")).then_inc(small_in, 16)
            sp.dma_start(w_uv[:, :], a["w_uv"].rearrange("a c h n -> (a c) (h n)")).then_inc(small_in, 16)
            sp.dma_start(kr_c[:, 2 * ROT:].rearrange("p (b r) -> p b r", r=ROT), kr_cache).then_inc(kr_in, 16)
            for b in range(CKV_SLOTS):
                sp.dma_start(ckv_c[:, b, :, :], ckv_cache[:, b, :, :]).then_inc(ckv_in[b], 16)

            def load_diff_k(b):
                sp.dma_start(dk_c[:, b % 2, :, :], dk_cache[:, b, :, :]).then_inc(dk_in[b % 2], 16)

            def load_diff_v(b):
                sp.dma_start(dv_c[:, b % 2, :, :], dv_cache[:, b, :, :]).then_inc(dv_in[b % 2], 16)

            def load_diff_new(b):
                sp.dma_start(newv[0:NEW, :], dv_s[b * NEW:(b + 1) * NEW, :]).then_inc(newv_in, 16)

            def load_latent_new(b):
                sp.dma_start(newckv[0:NEW, b % 2, :], ckv_s[b * NEW:(b + 1) * NEW, :]).then_inc(newckv_in[b % 2], 16)

            def load_stick_k(g, b):
                sp.dma_start(k_c[:, b % 2, :, :], sk_cache[:, b, :, g * GW:(g + 1) * GW]).then_inc(kc_in[b % 2], 16)

            def load_stick_v(g, b):
                sp.dma_start(v_c[:, b % 2, :, :], sv_cache[:, b, :, g * GW:(g + 1) * GW]).then_inc(vc_in[b % 2], 16)
                if b == 0:
                    sp.wait_ge(stored_v[g], 16)
                sp.dma_start(newv1[0:NEW, b % 2, :],
                             sv_s[b * NEW:(b + 1) * NEW, g * GW:(g + 1) * GW]).then_inc(vc_in[b % 2], 16)

            last_m = ("value", ("MS", STREAMS - 1))
            last_diff_score = [j for j in schedule if j[0] == "score2"][-1]
            last_value_before, last_samples_before = ("value", ("B", GROUPS - 2, PT_TILES - 1, GH - 1)), ("value", ("BS", GROUPS - 2, STREAMS // 2 - 1))

            def reload_x(tiles_):
                for t in tiles_:
                    src = x_p[:, t, :] if t < PT_TILES else x_s
                    sp.dma_start(x_sb[:, t, :], src).then_inc(xres_in[t], 16)

            for job in schedule:
                kind = job[0]
                if kind == "cvt" and job[1] + STAGES < QUARTERS * len(SECTIONS):
                    sp.wait_ge(cvt_done, job[1] + 1)
                    load_quarter(job[1] + STAGES)
                if kind == "latT" and job[1] == S_TILE:
                    sp.wait_ge(stored_ckv, 16 * 2)
                    for b in range(2):
                        load_latent_new(b)
                if kind == "value" and job[1][0] == "MS":
                    b = job[1][1] + 2
                    if b < STREAMS:
                        wait_filled(sp, job)
                        sp.dma_start(ckv_c[:, b % 2, :, :], ckv_cache[:, b, :, :]).then_inc(ckv_in[b % 2], 16)
                        load_latent_new(b)
                if job == last_m:
                    wait_filled(sp, job)
                    for b in range(2):
                        load_diff_k(b)
                        load_diff_v(b)
                    sp.wait_ge(stored_dv, 16)
                    load_diff_new(0)
                if job == ("om",):
                    wait_filled(sp, job)
                    for i, name in enumerate(("ln_even_g", "ln_even_b")):
                        sp.dma_start(gains[i], a[name].rearrange("a c -> (a c)").partition_broadcast(P)).then_inc(gains_in, 16)
                if kind == "cacheT" and job[1] == "DS" and job[3] == 1 and job[2] + 2 < STREAMS:
                    wait_filled(sp, job)
                    load_diff_k(job[2] + 2)
                if kind == "value" and job[1][0] == "DS":
                    wait_filled(sp, job)
                    if job[1][1] + 2 < STREAMS:
                        load_diff_v(job[1][1] + 2)
                    if job[1][1] + 1 < STREAMS:
                        load_diff_new(job[1][1] + 1)
                if job == last_diff_score:
                    wait_filled(sp, job)
                    reload_x(range(2))
                if kind == "ogT" and job[2] == 1 and job[1] in (0, 2, S_TILE):
                    wait_filled(sp, job)
                    reload_x([{0: 2, 2: 3, S_TILE: S_TILE}[job[1]]])
                if job == ("xT", 1, S_TILE, 1):
                    wait_drained(sp, job)
                    for b in range(2):
                        load_stick_k(0, b)
                if job == ("q", 0, 1, 1):
                    for b in range(2):
                        load_stick_v(0, b)
                if kind in ("cacheT", "value"):
                    stick = job[2:4] if job[1] == "BS" and job[4] == 1 else job[1][1:] if job[1][0] == "BS" else None
                    if stick:
                        g, pair = stick
                        g, pair = (g, pair + 1) if pair + 1 < STREAMS // 2 else (g + 1, 0)
                        if g < GROUPS:
                            wait_filled(sp, job)
                            for b in (2 * pair, 2 * pair + 1):
                                (load_stick_k if kind == "cacheT" else load_stick_v)(g, b)
                if job == ("ocvt", 3):
                    wait_filled(sp, last_value_before)
                    wait_filled(sp, last_samples_before)
                    sp.wait_ge(stored_vn[0], 16 * PT_TILES * GROUPS // 2)
                    sp.wait_ge(stored_v[GROUPS - 2], 16)
                    for i, name in enumerate(("ln_odd_g", "ln_odd_b")):
                        sp.dma_start(gains1[i], a[name].rearrange("a c -> (a c)").partition_broadcast(P)).then_inc(gains1_in, 16)

        @block.gpsimd
        def _(pool):
            nc.gpsimd.memset(minus_half[:, :], -0.5).then_inc(pool_step, 1)
            pool.wait_ge(pool_step, 1)
            total = 0
            for job in schedule:
                kind = job[0]
                if kind == "rms":
                    pool.wait_ge(pow_in, pow_no[job])
                    nc.gpsimd.tensor_tensor(ss[:, 2, :], ss[:, 1, :], minus_half[:, :], ALU.pow).then_inc(pow_out, 1)
                    pool.wait_ge(rms_done, 1)
                    pool.dma_start(ckv_s, lat[:, S_TILE, QL:QL + KVL]).then_inc(stored_ckv, 16)
                    pool.dma_start(kr_s, lat[:, S_TILE, QL + KVL:]).then_inc(stored_ckv, 16)
                    pool.wait_ge(stored_ckv, 32)
                    pool.dma_start(ckv_p, lat[:, 0:PT_TILES, QL:QL + KVL]).then_inc(stored_ckv, 16)
                    pool.dma_start(kr_p, lat[:, 0:PT_TILES, QL + KVL:]).then_inc(stored_ckv, 16)
                elif kind == "dk":
                    t = job[1]
                    pool.wait_ge(rot_done, rot_no[job])
                    pool.dma_start(dk_p[t] if t < PT_TILES else dk_s,
                                   rot[:, (rot_no[job] - 1) % 2, :]).then_inc(stored_rot[(rot_no[job] - 1) % 2], 16)
                elif kind == "dv" and job[2] == 1:
                    t = job[1]
                    wait_drained(pool, ("dv", t, 0))
                    wait_drained(pool, job)
                    if t < PT_TILES:
                        total += 16
                        pool.dma_start(dv_p[t], dv[:, t, :]).then_inc(stored, 16)
                    else:
                        pool.dma_start(dv_s, dv[:, t, :]).then_inc(stored_dv, 16)
                elif kind == "post":
                    pool.wait_ge(pow_in, pow_no[job])
                    nc.gpsimd.tensor_tensor(ss[:, 2, 0:DH], ss[:, 1, 0:DH], minus_half[:, 0:DH], ALU.pow).then_inc(pow_out, 1)
                elif kind == "ln":
                    i = ln_no[job] % 2
                    pool.wait_ge(pow_in, pow_no[job])
                    nc.gpsimd.tensor_tensor(rstd[:, i, :], mv[:, i, 1:2], minus_half[:, 0:1], ALU.pow).then_inc(pow_out, 1)
                elif kind == "shift":
                    _, layer, t = job
                    n = ln_no[("ln", layer, t)]
                    pool.wait_ge(gained, n)
                    pool.wait_ge(gains_in if layer == 0 else gains1_in, 32)
                    x_ = x_sb[:, t, :]
                    nc.gpsimd.tensor_tensor(x_, x_, (gains if layer == 0 else gains1)[1], ALU.add).then_inc(ln_done, 1)
                    if layer == 1:
                        pool.wait_ge(ln_done, n)
                        total += 16
                        pool.dma_start(y_p[t] if t < PT_TILES else y_s, x_sb[:, t, :]).then_inc(stored, 16)
                elif kind in ("k", "v"):
                    _, g, t = job
                    wait_drained(pool, job)
                    cols = slice(g * GW, (g + 1) * GW)
                    k_out, v_out = (sk_p[t], sv_p[t]) if t < PT_TILES else (sk_s, sv_s)
                    if kind == "k":
                        slot = (kn_no[job] - 1) % 2
                        pool.dma_start(k_out[:, cols], k_n[:, slot, :]).then_inc(stored_kn[slot], 16)
                    else:
                        pool.dma_start(v_out[:, cols], v_n[:, g % 2, t, :]).then_inc(
                            stored_vn[g % 2] if t < PT_TILES else stored_v[g], 16)
            pool.wait_ge(stored, total)
            pool.wait_ge(stored_ckv, 64)
            pool.wait_ge(stored_dv, 16)
            for g in range(GROUPS):
                pool.wait_ge(stored_v[g], 16)
            for i in range(2):
                pool.wait_ge(stored_kn[i], 16 * TILES * GROUPS // 2)
                pool.wait_ge(stored_vn[i], 16 * PT_TILES * GROUPS // 2)
            pool.wait_ge(stored_rot[0], 16 * 3)
            pool.wait_ge(stored_rot[1], 16 * 2)

        @block.tensor
        def _(pe):
            def mm(o, l, r, first, last):
                return nc.tensor.matmul(o, l, r, start=first, stop=last)

            def product(o, sta, mov, first, last):
                (s_hi, s_lo), (m_hi, m_lo) = sta, mov
                mm(o, s_hi, m_hi, first, False)
                mm(o, s_hi, m_lo, False, False)
                return mm(o, s_lo, m_hi, False, last)

            def x_block(k, cols):
                return xT_hi[:, k, cols], xT_lo[:, k, cols]

            def w_block(sec, c0, n):
                slot = SECTIONS.index(sec) % 2
                return w_hi[:, slot, c0:c0 + n], w_lo[:, slot, c0:c0 + n]

            def wait_quarter(job, sec, quarter):
                if units[sec][0] == job:
                    pe.wait_ge(cvt_done, QUARTERS * SECTIONS.index(sec) + quarter + 1)

            def project(job, t):
                wait_bank(pe, job)
                for i, sec in enumerate(sections_of(job)):
                    n = SEC_A - HALF if sec == "A1" else HALF
                    for k in range(KD):
                        wait_quarter(job, sec, k // 2)
                        m = product(ps(job)[:, i * HALF:i * HALF + n], x_block(k, tok(t)), w_block(sec, k * HALF, n),
                                    k == 0, k == KD - 1)
                m.then_inc(filled[where[job][0]], 1)

            def transposes(job, pieces):
                wait_bank(pe, job)
                for c0, src in pieces:
                    r, c = src.shape
                    i = nc.tensor.transpose(ps(job)[0:c, c0:c0 + r], src, ident[0:r, 0:r])
                i.then_inc(filled[where[job][0]], 1)

            pe.wait_ge(consts_in, 16)
            for job in schedule:
                kind = job[0]
                done = filled[where[job][0]] if job in where else None
                if kind == "xT":
                    _, layer, t, h = job
                    if layer == 0:
                        pe.wait_ge(x_in[t], 16)
                    else:
                        pe.wait_ge(ln_done, ln_no[("ln", 0, t)])
                    transposes(job, [(i * P, x_sb[:, t, (4 * h + i) * P:(4 * h + i + 1) * P]) for i in range(4)])
                elif kind == "A":
                    for h in range(2):
                        wait_drained(pe, ("xT", 0, job[1], h))
                    project(job, job[1])
                elif kind in ("G", "dq", "dk", "dv", "gd"):
                    project(job, job[1])
                elif kind == "latT":
                    t = job[1]
                    pe.wait_ge(rms_done, 1)
                    transposes(job, [(0, lat[:, t, 0:P]), (P, lat[:, t, P:2 * P]), (2 * P, lat[:, t, QL:QL + KVL]),
                                     (3 * P, lat[:, t, SEC_A - QK:SEC_A])])
                elif kind == "uq":
                    _, t, h = job
                    wait_drained(pe, ("latT", t))
                    pe.wait_ge(small_in, 16 * SMALL)
                    wait_bank(pe, job)
                    n = MH * QK // 2
                    for k in range(2):
                        i = mm(ps(job)[:, 0:n], latT[:, k, tok(t)], w_uq[:, k, h * n:(h + 1) * n], k == 0, k == 1)
                    i.then_inc(done, 1)
                elif kind == "qT":
                    _, t, h = job
                    pe.wait_ge(uq_done, t + 1)
                    transposes(job, [(i * P, uq[:, t % 2, (4 * h + i) * QK:(4 * h + i + 1) * QK]) for i in range(4)])
                elif kind == "kn":
                    h = job[1]
                    for t in range(PT_TILES):
                        wait_drained(pe, ("latT", t))
                    wait_bank(pe, job)
                    mm(ps(job)[0:NOPE, :], w_uk[:, h * NOPE:(h + 1) * NOPE], latT[:, 2, 0:SEQ], True, True).then_inc(done, 1)
                elif kind == "vm":
                    wait_bank(pe, job)
                    mm(ps(job)[:, :], latT[:, 2, tok(job[1])], w_uv[:, :], True, True).then_inc(done, 1)
                elif kind == "wukT":
                    transposes(job, [(i * P, w_uk[:, (4 * job[1] + i) * NOPE:(4 * job[1] + i + 1) * NOPE]) for i in range(4)])
                elif kind == "qa":
                    wait_drained(pe, ("wukT", job[1]))
                    wait_drained(pe, ("qT", S_TILE, job[1]))
                    wait_bank(pe, job)
                    for i in range(4):
                        h = 4 * job[1] + i
                        m = mm(ps(job)[:, i * P:(i + 1) * P], wukT[0:NOPE, h, :], qT[0:NOPE, h, tok(S_TILE)], True, True)
                    m.then_inc(done, 1)
                elif kind in ("dqT", "dkT"):
                    n = rot_no[(kind[:2], job[1])]
                    pe.wait_ge(rot_done, n)
                    transposes(job, [(i * P, rot[:, (n - 1) % 2, i * P:(i + 1) * P]) for i in range(4)])
                elif kind == "cacheT" and job[1] == "MS":
                    b = job[2]
                    pe.wait_ge(ckv_in[b % CKV_SLOTS], 16 * (b // CKV_SLOTS + 1))
                    pe.wait_ge(kr_in, 16)
                    pe.wait_ge(setup_done, 1)
                    wait_bank(pe, job)
                    for i in range(2):
                        nc.tensor.transpose(ps(job)[:, i * P:(i + 1) * P], ckv_c[:, b % CKV_SLOTS, i, :], ident[:, :])
                    for i in range(2):
                        m = nc.tensor.transpose(ps(job)[0:QK, (2 + i) * P:(3 + i) * P],
                                                kr_c[:, (2 * b + i) * ROT:(2 * b + i + 3) * ROT], ident[:, :])
                    m.then_inc(done, 1)
                elif kind == "cacheT" and job[1] == "DS":
                    b, half = job[2], job[3]
                    pe.wait_ge(dk_in[b % 2], 16 * (b // 2 + 1))
                    transposes(job, [(i * P, dk_c[:, b % 2, half, i * P:(i + 1) * P]) for i in range(4)])
                elif kind == "cacheT":
                    g, b = job[2], 2 * job[3] + job[4]
                    pe.wait_ge(kc_in[b % 2], 16 * (4 * g + b // 2 + 1))
                    transposes(job, [((2 * i + half) * P, k_c[:, b % 2, half, i * P:(i + 1) * P])
                                     for i in range(2) for half in range(2)])
                elif kind in ("score", "score2"):
                    s = job[1]
                    n = width(s)
                    wait_bank(pe, job)
                    o = ps(job)
                    if s[0] == "M":
                        _, t, h = s
                        for j in range(4):
                            wait_drained(pe, ("kn", h))
                            wait_drained(pe, ("latT", j))
                        for i in range(2):
                            wait_drained(pe, ("qT", t, i))
                        mm(o[:, 0:n], qT[0:QK, h, tok(t)], mlaK[0:QK, h, 0:n], True, False)
                        mm(o[:, n - P:n], identb[:, :], mask_chunk[:, :], False, True).then_inc(done, 1)
                    elif s[0] == "MS":
                        b = s[1]
                        wait_drained(pe, ("cacheT",) + s)
                        for i in range(2):
                            wait_drained(pe, ("qa", i))
                        qn, qrb = qa[:, b, :], qT[NOPE:QK, b, tok(S_TILE)]
                        mm(o[:, 0:PAST], qn, ckv_cT[:, b % 2, :], True, False)
                        mm(o[:, 0:PAST], qrb, kr_cT[NOPE:QK, b % 2, :], False, True)
                        mm(o[:, PAST:n], qn, ckvTs[:, b * NEW:(b + 1) * NEW], True, False)
                        mm(o[:, PAST:n], qrb, krTs[NOPE:QK, b * NEW:(b + 1) * NEW], False, True).then_inc(done, 1)
                    elif s[0] == "D":
                        _, t, h = s
                        r = slice(HD * (kind == "score2"), HD * (kind == "score2") + HD)
                        for j in range(t + 1):
                            wait_drained(pe, ("dkT", j))
                        wait_drained(pe, ("dqT", t))
                        mm(o[:, 0:n], dqT[r, h, tok(t)], dkT[r, h, 0:n], True, False)
                        mm(o[:, n - P:n], identb[:, :], mask_chunk[:, :], False, True).then_inc(done, 1)
                    elif s[0] == "DS":
                        b = s[1]
                        for i in range(2):
                            wait_drained(pe, ("cacheT",) + s + (i,))
                        wait_drained(pe, ("dkT", S_TILE))
                        pe.wait_ge(blocks_done, blocks_no[("qblocks",)])
                        for h in range(DH):
                            r = slice(2 * NEW * h, 2 * NEW * (h + 1))
                            mm(o[r, 0:PAST], qblk[:, b, h, :], dk_cT[:, b % 2, h, :], True, True)
                            m = mm(o[r, PAST:n], qblk[:, b, h, :], dkT[:, h, new(b)], True, True)
                        m.then_inc(done, 1)
                    elif s[0] == "B":
                        _, g, t, h = s
                        r = slice(HD * (h % 2), HD * (h % 2) + HD)
                        for j in range(t + 1):
                            wait_drained(pe, ("kT", g, j))
                        for part in range(2):
                            wait_drained(pe, ("q", g, h // 2, part))
                        mm(o[:, 0:n], qT1[r, g % 2, h // 2, tok(t)], kT[r, g % 2, h // 2, 0:n], True, False)
                        mm(o[:, n - P:n], identb[:, :], mask_causal[:, :], False, True).then_inc(done, 1)
                    else:
                        _, g, pair = s
                        wait_drained(pe, ("kT", g, S_TILE))
                        pe.wait_ge(blocks_done, blocks_no[("gblocks", g)])
                        for i in range(2):
                            b = 2 * pair + i
                            wait_drained(pe, ("cacheT",) + s + (i,))
                            r = slice(GH * NEW * i, GH * NEW * (i + 1))
                            for blk in range(2):
                                mm(o[r, 0:PAST], qblk1[:, b, blk, :], k_cT[:, b % 2, blk, :], blk == 0, blk == 1)
                            for blk in range(2):
                                mm(o[r, PAST:n], qblk1[:, b, blk, :], kT[:, g % 2, blk, new(b)], blk == 0, False)
                            m = mm(o[r, PAST:n], identb[:, r], mask_new[:, :], False, True)
                        m.then_inc(done, 1)
                elif kind == "turn":
                    s = job[1]
                    wait_bank(pe, job)
                    if s[0] == "M":
                        wait_drained(pe, ("score", s))
                    elif s in weigh_no:
                        pe.wait_ge(weigh_done, weigh_no[s])
                    else:
                        pe.wait_ge(stick_done, stick_no[s])
                    p = probs[:, nth[s] % 3, :]
                    for j, (k0, kn) in enumerate(turn_blocks(s)):
                        if s[0] == "DS":
                            m = mm(ps(job)[0:kn, j * DIFF_ROWS:(j + 1) * DIFF_ROWS], p[:, k0:k0 + kn],
                                   csel[:, s[1] % 2, :], True, True)
                        else:
                            m = nc.tensor.transpose(ps(job)[0:kn, j * P:(j + 1) * P], p[:, k0:k0 + kn], ident[:, :])
                    m.then_inc(done, 1)
                elif kind == "value":
                    s = job[1]
                    wait_bank(pe, job)
                    wait_drained(pe, ("turn", s))
                    o, w = ps(job), wT[:, nth[s] % 2, :]
                    blocks = turn_blocks(s)
                    last = len(blocks) - 1
                    if s[0] == "M":
                        h = s[2]
                        for j in range(last + 1):
                            wait_drained(pe, ("vm", j))
                            m = mm(o[:, 0:MV], w[:, tok(j)], vm[:, j, h * MV:(h + 1) * MV], j == 0, j == last)
                    elif s[0] == "MS":
                        b = s[1]
                        pe.wait_ge(newckv_in[b % 2], 16 * (b // 2 + 1))
                        for j in range(2):
                            mm(o[:, 0:P], ckv_c[:, b % CKV_SLOTS, j, :], w[:, tok(j)], j == 0, False)
                        m = mm(o[:, 0:P], newckv[0:NEW, b % 2, :], w[0:NEW, tok(2)], False, True)
                    elif s[0] == "D":
                        h = s[2]
                        for j in range(last + 1):
                            wait_drained(pe, ("dv", j, h // 2))
                            m = mm(o[:, 0:P], w[:, tok(j)], dv[:, j, h * P:(h + 1) * P], j == 0, j == last)
                    elif s[0] == "DS":
                        b = s[1]
                        pe.wait_ge(dv_in[b % 2], 16 * (b // 2 + 1))
                        pe.wait_ge(newv_in, 16 * (b + 1))
                        for h in range(DH):
                            c = slice(h * NEW, (h + 1) * NEW)
                            hc = slice(h * P, (h + 1) * P)
                            for j in range(2):
                                mm(o[:, c], dv_c[:, b % 2, j, hc], w[:, j * DIFF_ROWS + h * NEW:j * DIFF_ROWS + (h + 1) * NEW], j == 0, False)
                            m = mm(o[:, c], newv[0:NEW, hc],
                                   w[0:NEW, 2 * DIFF_ROWS + h * NEW:2 * DIFF_ROWS + (h + 1) * NEW], False, True)
                    elif s[0] == "B":
                        _, g, t, h = s
                        for j in range(last + 1):
                            wait_drained(pe, ("v", g, j))
                            m = mm(o[:, 0:HD], w[:, tok(j)], v_n[:, g % 2, j, h * HD:(h + 1) * HD], j == 0, j == last)
                    else:
                        _, g, pair = s
                        for i in range(2):
                            b = 2 * pair + i
                            pe.wait_ge(vc_in[b % 2], 32 * (4 * g + b // 2 + 1))
                            for blk in range(2):
                                c0 = (2 * i + blk) * 2 * NEW
                                oc, vc = o[:, c0:c0 + 2 * NEW], slice(blk * P, (blk + 1) * P)
                                for j in range(2):
                                    mm(oc, v_c[:, b % 2, j, vc], w[:, j * P + c0:j * P + c0 + 2 * NEW], j == 0, False)
                                m = mm(oc, newv1[0:NEW, b % 2, vc], w[0:NEW, 2 * P + c0:2 * P + c0 + 2 * NEW], False, True)
                    m.then_inc(done, 1)
                elif kind == "om":
                    wait_drained(pe, ("value", ("MS", STREAMS - 1)))
                    wait_bank(pe, job)
                    for h in range(MH):
                        m = mm(ps(job)[:, h * MV:(h + 1) * MV], o_mlaT[:, h, :], w_uv[:, h * MV:(h + 1) * MV], True, True)
                    m.then_inc(done, 1)
                elif kind == "od":
                    wait_drained(pe, ("value", ("DS", STREAMS - 1)))
                    transposes(job, [(h * P, od_T[:, h, :]) for h in range(DH)])
                elif kind == "ogT":
                    _, t, h = job
                    if h == 0:
                        wait_drained(pe, ("value", ("M", t, MH - 1)) if t < PT_TILES else ("om",))
                    else:
                        pe.wait_ge(post_done, t + 1)
                    src = gates if h == 0 else od_n
                    transposes(job, [(i * P, src[:, t, i * P:(i + 1) * P]) for i in range(4)])
                elif kind == "out":
                    _, layer, part, t, h = job
                    if layer == 0:
                        wait_drained(pe, ("ogT", t, part))
                    else:
                        pe.wait_ge(ocvt_done, ocvt_no[("ocvt", 4 * part + 3 if part == 0 else 5)])
                        if part == last_part(layer, t) and t < PT_TILES:
                            wait_drained(pe, ("oT", GROUPS - 1, t))
                        elif part == 2:
                            pe.wait_ge(ocvt_done, ocvt_no[("ocvt", "samples")])
                    wait_bank(pe, job)
                    sec = sections_of(job)[0]
                    ks = out_blocks(job)
                    for k in ks:
                        wait_quarter(job, sec, k % 4)
                        m = product(ps(job)[:, :], x_block(k, tok(t)), w_block(sec, k % 4 * 512, 512), k == ks[0], k == ks[-1])
                    m.then_inc(done, 1)
                elif kind in ("k", "v", "g"):
                    _, g, t = job
                    for h in range(2):
                        wait_drained(pe, ("xT", 1, t, h))
                    project(job, t)
                elif kind == "kT":
                    _, g, t = job
                    wait_drained(pe, ("k", g, t))
                    transposes(job, [(i * P, k_n[:, (kn_no[("k", g, t)] - 1) % 2, i * P:(i + 1) * P]) for i in range(2)])
                elif kind == "q":
                    _, g, blk, part = job
                    wait_bank(pe, job)
                    sec = sections_of(job)[0]
                    for k in range(KD):
                        wait_quarter(job, sec, k // 2)
                        m = product(ps(job)[:, 0:TOK // 2], w_block(sec, k * HALF + blk * P, P),
                                    x_block(k, slice(part * TOK // 2, (part + 1) * TOK // 2)), k == 0, k == KD - 1)
                    m.then_inc(done, 1)
                elif kind == "gsT":
                    g = job[1]
                    wait_drained(pe, ("g", g, S_TILE))
                    e = gtmp[:, (gate_no[("g", g, S_TILE)] - 1) % 2, :]
                    transposes(job, [(i * P, e[:, i * P:(i + 1) * P]) for i in range(2)])
                elif kind == "oT":
                    _, g, t = job
                    wait_drained(pe, ("value", ("B", g, t, GH - 1)))
                    transposes(job, [(i * P, g1[:, g % 2, t, i * P:(i + 1) * P]) for i in range(2)])

        def transposed(job):
            if job[0] == "oT":
                ks, t = slice(2 * job[1], 2 * job[1] + 2), job[2]
            else:
                h, t = (job[3], job[2]) if job[0] == "xT" else (job[2], job[1])
                ks = slice(4 * h, 4 * h + 4)
            n = ks.stop - ks.start
            return (lambda buf: buf[:, ks, tok(t)]), ps(job)[:, 0:n * P].rearrange("p (k n) -> p k n", k=n)

        def words_of(n):
            if SECTIONS[n // QUARTERS] != "A1":
                return lambda buf: buf
            return lambda buf: buf.rearrange("p (k c) -> p k c", k=2)[:, :, 0:SEC_A - HALF]

        def wait_heads(eng, job):
            g = GROUPS - 1 if job[1] == "samples" else job[1] // 2
            if job[1] != "samples":
                wait_filled(eng, units[f"g{GROUPS - 1}"][1])
                for t in range(PT_TILES):
                    wait_drained(eng, ("oT", g, t))
            wait_drained(eng, ("value", ("BS", g, STREAMS // 2 - 1)))

        @block.scalar
        def _(act):
            steps_done = [0]

            def link(ins):
                steps_done[0] += 1
                ins.then_inc(act_step, 1)
                act.wait_ge(act_step, steps_done[0])

            for job in schedule:
                kind = job[0]
                done = drained[where[job][0]] if job in where else None
                if job in two_parts_no:
                    dst, src = transposed(job)
                    wait_filled(act, job)
                    nc.scalar.copy(dst(xT_hi), src).then_inc(xhi_done, 1)
                elif kind == "cvt":
                    n = job[1]
                    sec, k = n // QUARTERS, n % QUARTERS
                    if k == 0 and sec >= 2:
                        wait_filled(act, units[SECTIONS[sec - 2]][1])
                    act.wait_ge(stage_in[n % STAGES], 16 * (n // STAGES + 1))
                    piece = words_of(n)
                    nc.scalar.copy(piece(w_hi[:, sec % 2, k * 512:(k + 1) * 512]), piece(stage[:, n % STAGES, :])).then_inc(hi_done, 1)
                elif kind == "ocvt":
                    ks, cols = (slice(6, 8), tok(S_TILE)) if job[1] == "samples" else (slice(job[1], job[1] + 1), slice(0, TOK))
                    wait_heads(act, job)
                    nc.scalar.copy(xT_hi[:, ks, cols], oT[:, ks, cols]).then_inc(ocvt_hi, 1)
                elif kind == "A":
                    wait_filled(act, job)
                    cols = slice(0, HALF) if job[2] == 0 else slice(HALF, SEC_A)
                    nc.scalar.copy(lat[:, job[1], cols], ps(job)[:, 0:cols.stop - cols.start]).then_inc(done, 1)
                elif kind == "G":
                    wait_filled(act, job)
                    nc.scalar.activation(gates[:, job[1], job[2] * HALF:(job[2] + 1) * HALF], ps(job)[:, 0:HALF], ACT.Silu).then_inc(done, 1)
                elif kind == "gd":
                    wait_filled(act, job)
                    if job[1] == 0:
                        wait_filled(act, ("dqT", PT_TILES - 1))
                    if job[1] >= 2:
                        act.wait_ge(post_done, job[1] - 1)
                    nc.scalar.activation(rot[:, job[1] % 2, :], ps(job)[:, :], ACT.Silu).then_inc(done, 1)
                elif kind == "uq":
                    _, t, h = job
                    wait_filled(act, job)
                    n = MH * QK // 2
                    nc.scalar.copy(uq[:, t % 2, h * n:(h + 1) * n], ps(job)[:, 0:n]).then_inc(done, 1)
                elif kind == "qT":
                    _, t, h = job
                    wait_filled(act, job)
                    src = ps(job)[:, :].rearrange("p (k n) -> p k n", k=4)
                    if t < PT_TILES:
                        nc.scalar.mul(qT[0:QK, 4 * h:4 * h + 4, tok(t)], src[0:QK], MLA_SCALE).then_inc(done, 1)
                    else:
                        nc.scalar.mul(qT[0:NOPE, 4 * h:4 * h + 4, tok(t)], src[0:NOPE], MLA_SCALE)
                        nc.scalar.mul(
                            qT[NOPE:QK, :, SEQ + 4 * h * NEW:SEQ + 4 * (h + 1) * NEW].rearrange("p b (h q) -> p b h q", h=4),
                            ps(job)[NOPE:QK, :].rearrange("p (h b q) -> p b h q", h=4, q=NEW), MLA_SCALE).then_inc(done, 1)
                elif kind == "vm":
                    wait_filled(act, job)
                    nc.scalar.copy(vm[:, job[1], :], ps(job)[:, :]).then_inc(done, 1)
                elif kind == "qa":
                    wait_filled(act, job)
                    half = slice(4 * job[1] * NEW, 4 * (job[1] + 1) * NEW)
                    nc.scalar.copy(qa[:, :, half].rearrange("p b (h q) -> p h b q", h=4),
                                   ps(job)[:, :].rearrange("p (h b q) -> p h b q", h=4, q=NEW)).then_inc(done, 1)
                elif kind in ("dq", "dk"):
                    n = rot_no[job] - 1
                    wait_filled(act, job)
                    if n >= 2 and (kind == "dk" or n < TILES + 2):
                        act.wait_ge(stored_rot[n % 2], 16 * (n // 2))
                    nc.scalar.copy(rot[:, n % 2, :], ps(job)[:, :]).then_inc(done, 1)
                elif kind == "dqT":
                    wait_filled(act, job)
                    nc.scalar.mul(dqT[:, :, tok(job[1])],
                                  ps(job)[:, :].rearrange("p (k n) -> p k n", k=4), HEAD_SCALE).then_inc(done, 1)
                elif kind == "dv":
                    wait_filled(act, job)
                    nc.scalar.copy(dv[:, job[1], job[2] * HALF:(job[2] + 1) * HALF], ps(job)[:, 0:HALF]).then_inc(done, 1)
                elif kind == "cacheT" and job[1] == "DS" or kind == "cacheT" and job[1] == "BS" and job[4] == 0:
                    wait_filled(act, job)
                    src = ps(job)[:, :].rearrange("p (k n) -> p k n", k=4)
                    if job[1] == "DS":
                        nc.scalar.copy(dk_cT[:, job[2] % 2, :, tok(job[3])], src).then_inc(done, 1)
                    else:
                        nc.scalar.copy(k_cT[:, 0, :, :].rearrange("p a b -> p (a b)"), ps(job)[:, :]).then_inc(done, 1)
                elif kind in ("score", "score2") and ("score", job[1]) in exp_no:
                    s = job[1]
                    act.wait_ge(max_done, exp_no[job])
                    r = nth[s] % 8
                    p, st = (probs[:, nth[s] % 3, :], stats) if kind == "score" else (probs2[:, nth[s] % 2, :], stats2)
                    nc.scalar.activation(p[:, 0:width(s)], ps(job)[:, 0:width(s)], ACT.Exp, bias=st[:, 0, r:r + 1],
                                         accum_out=st[:, 1, r:r + 1]).then_inc(done, 1)
                elif kind == "score":
                    s = job[1]
                    e = soft[:, nth[s] % 2, 0:width(s)]
                    wait_filled(act, job)
                    link(nc.scalar.activation(e, ps(job)[:, 0:width(s)], ACT.Abs))
                    link(nc.scalar.activation(e, e, ACT.Exp, scale=-1.0))
                    nc.scalar.activation(e, e, ACT.Ln, bias=1.0).then_inc(soft_done, 1)
                elif kind == "weigh" and job[1] in stick_no:
                    s = job[1]
                    p = probs[:, nth[s] % 3, 0:width(s)]
                    wait_drained(act, ("score", s))
                    nc.scalar.activation(p, p, ACT.Exp).then_inc(stick_done, 1)
                elif kind == "value" and job[1][0] in ("MS", "DS"):
                    s = job[1]
                    wait_filled(act, job)
                    if s[0] == "MS":
                        nc.scalar.copy(o_mlaT[:, :, s[1] * NEW:(s[1] + 1) * NEW],
                                       ps(job)[:, 0:P].rearrange("p (h q) -> p h q", h=MH)).then_inc(done, 1)
                    else:
                        nc.scalar.copy(od_T[:, :, s[1] * NEW:(s[1] + 1) * NEW],
                                       ps(job)[:, 0:DIFF_ROWS].rearrange("p (h q) -> p h q", h=DH)).then_inc(done, 1)
                elif kind == "od":
                    wait_filled(act, job)
                    nc.scalar.copy(od_n[:, S_TILE, :], ps(job)[:, :]).then_inc(done, 1)
                elif kind == "lam":
                    act.wait_ge(dve_lam, 1)
                    nc.scalar.activation(lam[:, 2:4], lam[:, 0:2], ACT.Exp).then_inc(act_lam, 1)
                elif kind == "k":
                    _, g, t = job
                    if g == 0 and t == 0:
                        nc.scalar.preload_act_table_set("natural_log_exp_and_others")
                    wait_filled(act, job)
                    n = kn_no[job] - 1
                    if n >= 2:
                        act.wait_ge(stored_kn[n % 2], 16 * (n // 2))
                    nc.scalar.copy(k_n[:, n % 2, :], ps(job)[:, 0:GW]).then_inc(done, 1)
                elif kind == "v":
                    _, g, t = job
                    wait_filled(act, job)
                    if g >= 2 and t == 0:
                        act.wait_ge(stored_vn[g % 2], 16 * PT_TILES * (g // 2))
                        act.wait_ge(stored_v[g - 2], 16)
                    nc.scalar.copy(v_n[:, g % 2, t, :], ps(job)[:, 0:GW]).then_inc(done, 1)
                elif kind == "q":
                    _, g, blk, part = job
                    wait_filled(act, job)
                    nc.scalar.mul(qT1[:, g % 2, blk, part * TOK // 2:(part + 1) * TOK // 2], ps(job)[:, 0:TOK // 2],
                                  HEAD_SCALE).then_inc(done, 1)
                elif kind == "g":
                    wait_filled(act, job)
                    if job[2] == 1:
                        wait_filled(act, ("gsT", job[1]))
                    nc.scalar.activation(gtmp[:, (gate_no[job] - 1) % 2, :], ps(job)[:, 0:GW], ACT.Exp, scale=-1.0).then_inc(gate_e, 1)
                elif kind == "shift":
                    n = ln_no[("ln",) + job[1:]]
                    x_, i = x_sb[:, job[2], :], n % 2
                    act.wait_ge(scale_done, n)
                    nc.scalar.activation(x_, x_, ACT.Identity, bias=mv[:, i, 0:1], scale=rstd[:, i, :]).then_inc(norm_done, 1)

        @block.vector
        def _(dve):
            v = nc.vector
            steps_done = [0]

            def link(ins):
                steps_done[0] += 1
                ins.then_inc(dve_step, 1)
                dve.wait_ge(dve_step, steps_done[0])

            def rotate(x1, x2, cos, sin, t1, t2):
                v.tensor_tensor(t1, x1, sin, ALU.mult)
                link(v.tensor_tensor(t2, x2, sin, ALU.mult))
                v.tensor_tensor(x1, x1, cos, ALU.mult)
                link(v.tensor_tensor(x2, x2, cos, ALU.mult))
                link(v.tensor_tensor(x1, x1, t2, ALU.subtract))
                return v.tensor_tensor(x2, x2, t1, ALU.add)

            v.memset(kr_c[:, 0:2 * ROT], 0.0).then_inc(setup_done, 1)
            for job in schedule:
                kind = job[0]
                done = drained[where[job][0]] if job in where else None
                if job in two_parts_no:
                    dst, src = transposed(job)
                    dve.wait_ge(xhi_done, two_parts_no[job])
                    v.tensor_tensor(dst(xT_lo), src, dst(xT_hi).bitcast(F32), ALU.subtract).then_inc(done, 1)
                elif kind == "cvt":
                    n = job[1]
                    sec, k = n // QUARTERS, n % QUARTERS
                    piece, words = words_of(n), slice(k * 512, (k + 1) * 512)
                    dve.wait_ge(hi_done, n + 1)
                    v.tensor_tensor(piece(w_lo[:, sec % 2, words]), piece(stage[:, n % STAGES, :]),
                                    piece(w_hi[:, sec % 2, words].bitcast(F32)), ALU.subtract).then_inc(cvt_done, 1)
                elif kind == "ocvt":
                    ks, cols = (slice(6, 8), tok(S_TILE)) if job[1] == "samples" else (slice(job[1], job[1] + 1), slice(0, TOK))
                    dve.wait_ge(ocvt_hi, ocvt_no[job])
                    v.tensor_tensor(xT_lo[:, ks, cols], oT[:, ks, cols], xT_hi[:, ks, cols].bitcast(F32),
                                    ALU.subtract).then_inc(ocvt_done, 1)
                elif kind == "rms":
                    dve.wait_ge(small_in, 16 * SMALL)
                    for t in range(TILES):
                        for h in range(2):
                            wait_drained(dve, ("A", t, h))
                    q_, c_ = lat[:, :, 0:QL], lat[:, :, QL:QL + KVL]
                    sq_q = sq[:, 0:TILES * QL].rearrange("p (t c) -> p t c", t=TILES)
                    sq_c = sq[:, TILES * QL:TILES * (QL + KVL)].rearrange("p (t c) -> p t c", t=TILES)
                    v.tensor_tensor(sq_q, q_, q_, ALU.mult)
                    link(v.tensor_tensor(sq_c, c_, c_, ALU.mult))
                    v.tensor_reduce(ss[:, 0, 0:TILES], sq_q, AX_X, ALU.add)
                    link(v.tensor_reduce(ss[:, 0, TILES:], sq_c, AX_X, ALU.add))
                    v.tensor_scalar(ss[:, 1, 0:TILES], ss[:, 0, 0:TILES], 1.0 / QL, EPS, ALU.mult, ALU.add)
                    v.tensor_scalar(ss[:, 1, TILES:], ss[:, 0, TILES:], 1.0 / KVL, EPS, ALU.mult, ALU.add).then_inc(pow_in, 1)
                    dve.wait_ge(pow_out, pow_no[job])
                    v.tensor_tensor(q_, q_, ss[:, 2, 0:TILES].unsqueeze(2).broadcast_to([P, TILES, QL]), ALU.mult)
                    link(v.tensor_tensor(c_, c_, ss[:, 2, TILES:].unsqueeze(2).broadcast_to([P, TILES, KVL]), ALU.mult))
                    v.tensor_tensor(q_, q_, g_q[:, :].unsqueeze(1).broadcast_to([P, TILES, QL]), ALU.mult)
                    v.tensor_tensor(c_, c_, g_kv[:, :].unsqueeze(1).broadcast_to([P, TILES, KVL]), ALU.mult)
                    half = ROT // 2
                    k_ = lat[:, :, QL + KVL:]
                    t1 = sq[:, 2000:2000 + TILES * half].rearrange("p (t c) -> p t c", t=TILES)
                    t2 = sq[:, 2100:2100 + TILES * half].rearrange("p (t c) -> p t c", t=TILES)
                    rotate(k_[:, :, 0:half], k_[:, :, half:], ropem[:, :, 0:half], ropem[:, :, half:], t1, t2).then_inc(rms_done, 1)
                elif kind == "lam":
                    dve.wait_ge(small_in, 16 * SMALL)
                    dve.wait_ge(consts_in, 16)
                    v.tensor_copy(identb[:, :], ident[:, :])
                    v.tensor_copy(mask_chunk[:, :], probs[:, 0, 0:P])
                    v.tensor_copy(mask_causal[:, :], probs[:, 0, P:2 * P])
                    v.tensor_copy(mask_new[:, :], probs[:, 0, 2 * P:MASKS])
                    link(v.tensor_tensor(lam4[:, 0:2, :], lam4[:, 0:2, :], lam4[:, 2:4, :], ALU.mult))
                    v.tensor_reduce(lam[:, 0:2], lam4[:, 0:2, :], AX_X, ALU.add).then_inc(dve_lam, 1)
                    dve.wait_ge(act_lam, 1)
                    link(v.tensor_tensor(lam[:, 4:5], lam[:, 3:4], lam[:, 2:3], ALU.subtract))
                    link(v.tensor_scalar(lam[:, 5:6], lam[:, 4:5], -LAM_INIT, None, ALU.add))
                    link(v.tensor_scalar(sign[:, 1:2], sign[:, 1:2], lam[:, 5:6], None, ALU.mult))
                    link(v.tensor_tensor(sign[:, 0:1], sign[:, 0:1], sign[:, 1:2], ALU.add))
                    link(v.tensor_scalar(g_sub[:, :], g_sub[:, :], 1.0 - LAM_INIT, None, ALU.mult))
                elif kind == "latT":
                    t = job[1]
                    wait_filled(dve, job)
                    v.tensor_copy(latT[:, :, tok(t)], ps(job)[:, 0:3 * P].rearrange("p (k n) -> p k n", k=3))
                    kr = ps(job)[NOPE:QK, 3 * P:]
                    if t < PT_TILES:
                        v.tensor_copy(mlaK[NOPE:QK, :, tok(t)], kr.unsqueeze(1).broadcast_to([ROT, MH, P])).then_inc(done, 1)
                    else:
                        v.tensor_copy(ckvTs[:, :], ps(job)[:, 2 * P:3 * P])
                        v.tensor_copy(krTs[NOPE:QK, :], kr).then_inc(done, 1)
                elif kind == "uqrope":
                    t = job[1]
                    for h in range(2):
                        wait_drained(dve, ("uq", t, h))
                    if t:
                        dve.wait_ge(uq_done, t)
                    q_ = uq[:, t % 2, :].rearrange("p (h c) -> p h c", h=MH)
                    half = ROT // 2
                    cos = ropem[:, t:t + 1, 0:half].broadcast_to([P, MH, half])
                    sin = ropem[:, t:t + 1, half:].broadcast_to([P, MH, half])
                    t1, t2 = (rtmp[:, i, :].rearrange("p (h c) -> p h c", h=MH) for i in range(2))
                    rotate(q_[:, :, NOPE:NOPE + half], q_[:, :, NOPE + half:], cos, sin, t1, t2).then_inc(uq_done, 1)
                elif kind == "kn":
                    wait_filled(dve, job)
                    v.tensor_copy(mlaK[0:NOPE, job[1], :], ps(job)[0:NOPE, :]).then_inc(done, 1)
                elif kind == "wukT":
                    wait_filled(dve, job)
                    v.tensor_copy(wukT[0:NOPE, 4 * job[1]:4 * job[1] + 4, :],
                                  ps(job)[0:NOPE, :].rearrange("p (k n) -> p k n", k=4)).then_inc(done, 1)
                elif kind in ("dq", "dk"):
                    t, n = job[1], rot_no[job] - 1
                    wait_drained(dve, job)
                    if n:
                        dve.wait_ge(rot_done, n)
                    else:
                        dve.wait_ge(uq_done, TILES)
                    q_ = rot[:, n % 2, :].rearrange("p (h c) -> p h c", h=2 * DH)
                    half = DROT // 2
                    cos = roped[:, t:t + 1, 0:half].broadcast_to([P, 2 * DH, half])
                    sin = roped[:, t:t + 1, half:].broadcast_to([P, 2 * DH, half])
                    t1, t2 = (rtmp[:, i, 0:2 * DH * half].rearrange("p (h c) -> p h c", h=2 * DH) for i in range(2))
                    rotate(q_[:, :, 0:half], q_[:, :, half:DROT], cos, sin, t1, t2).then_inc(rot_done, 1)
                elif kind == "dkT":
                    wait_filled(dve, job)
                    v.tensor_copy(dkT[:, :, tok(job[1])], ps(job)[:, :].rearrange("p (k n) -> p k n", k=4)).then_inc(done, 1)
                elif kind == "cacheT" and job[1] == "MS":
                    b = job[2]
                    wait_filled(dve, job)
                    dve.wait_ge(stored_ckv, 16 * 4)
                    v.tensor_copy(ckv_cT[:, b % 2, :], ps(job)[:, 0:PAST])
                    v.tensor_copy(kr_cT[NOPE:QK, b % 2, :], ps(job)[NOPE:QK, PAST:]).then_inc(done, 1)
                elif kind == "cacheT" and job[1] == "BS" and job[4] == 1:
                    wait_filled(dve, job)
                    v.tensor_copy(k_cT[:, 1, :, :].rearrange("p a b -> p (a b)"), ps(job)[:, :]).then_inc(done, 1)
                elif kind in ("score", "score2") and ("score", job[1]) in exp_no:
                    s = job[1]
                    st = stats if kind == "score" else stats2
                    r = nth[s] % 8
                    wait_filled(dve, job)
                    v.tensor_reduce(st[:, 0, r:r + 1], ps(job)[:, 0:width(s)], AX_X, ALU.max, negate=True).then_inc(max_done, 1)
                elif kind == "score":
                    s = job[1]
                    n = width(s)
                    z = ps(job)[:, 0:n]
                    e = soft[:, nth[s] % 2, 0:n]
                    dve.wait_ge(soft_done, stick_no[s])
                    link(v.scalar_tensor_tensor(out=e, in0=z, scalar=0.0, in1=e, op0=ALU.max, op1=ALU.add))
                    link(v.tensor_tensor_scan(cum[:, 0:n][:, ::-1], e[:, ::-1], e[:, ::-1], 0.0, ALU.add, ALU.max))
                    v.tensor_tensor(probs[:, nth[s] % 3, 0:n], z, cum[:, 0:n], ALU.subtract).then_inc(done, 1)
                elif kind == "weigh" and job[1] in weigh_no:
                    s = job[1]
                    n, r = width(s), nth[s] % 8
                    p = probs[:, nth[s] % 3, 0:n]
                    wait_drained(dve, ("score", s))
                    if s[0] == "D":
                        wait_drained(dve, ("score2", s))
                    link(v.reciprocal(coef[:, 0, r:r + 1], stats[:, 1, r:r + 1]))
                    if s[0] == "MS":
                        v.tensor_scalar(p, p, coef[:, 0, r:r + 1], None, ALU.mult).then_inc(weigh_done, 1)
                    elif s[0] == "D":
                        p2 = probs2[:, nth[s] % 2, 0:n]
                        link(v.reciprocal(coef[:, 1, r:r + 1], stats2[:, 1, r:r + 1]))
                        link(v.tensor_scalar(p2, p2, coef[:, 1, r:r + 1], lam[:, 5:6], ALU.mult, ALU.mult))
                        v.scalar_tensor_tensor(out=p, in0=p, scalar=coef[:, 0, r:r + 1], in1=p2,
                                               op0=ALU.mult, op1=ALU.add).then_inc(weigh_done, 1)
                    else:
                        v.tensor_scalar(csel[:, s[1] % 2, :], sel[:, :], coef[:, 0, r:r + 1], sign[:, 0:1],
                                        ALU.mult, ALU.mult).then_inc(weigh_done, 1)
                elif kind == "turn":
                    s = job[1]
                    w = wT[:, nth[s] % 2, :]
                    m = DIFF_ROWS if s[0] == "DS" else P
                    wait_filled(dve, job)
                    if s[0] in ("M", "D", "B"):
                        v.tensor_copy(w[:, 0:width(s)], ps(job)[:, 0:width(s)]).then_inc(done, 1)
                    else:
                        v.tensor_copy(w[:, 0:2 * m], ps(job)[:, 0:2 * m])
                        v.tensor_copy(w[0:NEW, 2 * m:3 * m], ps(job)[0:NEW, 2 * m:3 * m]).then_inc(done, 1)
                elif kind == "value" and job[1][0] == "M":
                    s = job[1]
                    _, t, h = s
                    r = nth[s] % 8
                    wait_filled(dve, job)
                    wait_drained(dve, ("G", t, h // 4))
                    wait_drained(dve, ("score", s))
                    link(v.reciprocal(coef[:, 0, r:r + 1], stats[:, 1, r:r + 1]))
                    g_ = gates[:, t, h * MV:(h + 1) * MV]
                    v.scalar_tensor_tensor(out=g_, in0=ps(job)[:, 0:MV], scalar=coef[:, 0, r:r + 1], in1=g_,
                                           op0=ALU.mult, op1=ALU.mult).then_inc(done, 1)
                elif kind == "value" and job[1][0] == "D":
                    _, t, h = job[1]
                    wait_filled(dve, job)
                    v.tensor_copy(od_n[:, t, h * P:(h + 1) * P], ps(job)[:, 0:P]).then_inc(done, 1)
                elif kind == "value" and job[1][0] == "B":
                    _, g, t, h = job[1]
                    wait_filled(dve, job)
                    g_ = g1[:, g % 2, t, h * HD:(h + 1) * HD]
                    v.tensor_tensor(g_, ps(job)[:, 0:HD], g_, ALU.mult).then_inc(done, 1)
                elif kind == "value" and job[1][0] == "BS":
                    _, g, pair = job[1]
                    wait_filled(dve, job)
                    o = ps(job)[:, 0:P].rearrange("p (i k q) -> p k i q", i=2, k=2)
                    for par in range(2):
                        r = slice(HD * par, HD * (par + 1))
                        i = v.tensor_tensor(
                            oT[r, 2 * g:2 * g + 2, SEQ + 2 * pair * NEW:SEQ + 2 * (pair + 1) * NEW].rearrange("p k (i q) -> p k i q", i=2),
                            o[r, :, :, par * NEW:(par + 1) * NEW],
                            gsT[r, g % 2, :, 2 * pair * NEW:2 * (pair + 1) * NEW].rearrange("p k (i q) -> p k i q", i=2), ALU.mult)
                    i.then_inc(done, 1)
                elif kind == "om":
                    wait_filled(dve, job)
                    g_ = gates[:, S_TILE, :]
                    v.tensor_tensor(g_, ps(job)[:, :], g_, ALU.mult).then_inc(done, 1)
                elif kind == "clear":
                    link(v.memset(qblk[:, :, :, :], 0.0))
                elif kind == "qblocks":
                    wait_drained(dve, ("dqT", S_TILE))
                    for h in range(DH):
                        for i in range(2):
                            r = slice(HD * i, HD * (i + 1))
                            ins = v.tensor_copy(qblk[r, :, h, i * NEW:(i + 1) * NEW],
                                                dqT[r, h, tok(S_TILE)].rearrange("p (b q) -> p b q", b=STREAMS))
                    ins.then_inc(blocks_done, 1)
                elif kind == "post":
                    t = job[1]
                    o = od_n[:, t, :]
                    if t < PT_TILES:
                        wait_drained(dve, ("value", ("D", t, DH - 1)))
                    else:
                        wait_drained(dve, ("od",))
                    o3 = o.rearrange("p (h c) -> p h c", h=DH)
                    s3 = sq2.rearrange("p (h c) -> p h c", h=DH)
                    link(v.tensor_tensor(sq2, o, o, ALU.mult))
                    link(v.tensor_reduce(ss[:, 0, 0:DH], s3, AX_X, ALU.add))
                    v.tensor_scalar(ss[:, 1, 0:DH], ss[:, 0, 0:DH], 1.0 / (2 * HD), EPS, ALU.mult, ALU.add).then_inc(pow_in, 1)
                    link(v.tensor_tensor(o3, o3, g_sub[:, :].unsqueeze(1).broadcast_to([P, DH, 2 * HD]), ALU.mult))
                    dve.wait_ge(pow_out, pow_no[job])
                    link(v.tensor_tensor(o3, o3, ss[:, 2, 0:DH].unsqueeze(2).broadcast_to([P, DH, 2 * HD]), ALU.mult))
                elif kind == "gate":
                    t = job[1]
                    wait_drained(dve, ("gd", t))
                    v.tensor_tensor(od_n[:, t, :], od_n[:, t, :], rot[:, t % 2, :], ALU.mult).then_inc(post_done, 1)
                elif kind == "out":
                    _, layer, part, t, h = job
                    x_ = x_sb[:, t, h * 512:(h + 1) * 512]
                    if part == 0:
                        if layer == 0:
                            dve.wait_ge(xres_in[t], 16)
                        wait_filled(dve, job)
                        v.scalar_tensor_tensor(out=x_, in0=x_, scalar=ALPHA, in1=ps(job)[:, :], op0=ALU.mult,
                                               op1=ALU.add).then_inc(done, 1)
                    else:
                        wait_drained(dve, ("out", layer, part - 1, t, h))
                        wait_filled(dve, job)
                        v.tensor_tensor(x_, x_, ps(job)[:, :], ALU.add).then_inc(done, 1)
                elif kind == "ln":
                    _, layer, t = job
                    x_, i = x_sb[:, t, :], ln_no[job] % 2
                    for h in range(2):
                        wait_drained(dve, ("out", layer, last_part(layer, t), t, h))
                    v.bn_stats(bn[:, 0, :], x_[:, 0:512])
                    link(v.bn_stats(bn[:, 1, :], x_[:, 512:]))
                    link(v.bn_aggr(mv[:, i, :], bn[:, :, :]))
                    v.tensor_scalar(mv[:, i, 1:2], mv[:, i, 1:2], EPS, None, ALU.add).then_inc(pow_in, 1)
                elif kind == "shift":
                    _, layer, t = job
                    x_, n = x_sb[:, t, :], ln_no[("ln", layer, t)]
                    dve.wait_ge(pow_out, pow_no[("ln", layer, t)])
                    v.scalar_tensor_tensor(out=mv[:, n % 2, 0:1], in0=mv[:, n % 2, 0:1], scalar=-1.0, in1=rstd[:, n % 2, :],
                                           op0=ALU.mult, op1=ALU.mult).then_inc(scale_done, 1)
                    dve.wait_ge(gains_in if layer == 0 else gains1_in, 32)
                    dve.wait_ge(norm_done, n)
                    v.tensor_tensor(x_, x_, (gains if layer == 0 else gains1)[0], ALU.mult).then_inc(gained, 1)
                elif kind == "kT":
                    _, g, t = job
                    wait_filled(dve, job)
                    v.tensor_copy(kT[:, g % 2, :, tok(t)], ps(job)[:, 0:2 * P].rearrange("p (k n) -> p k n", k=2)).then_inc(done, 1)
                elif kind == "gblocks":
                    g = job[1]
                    if g == 0:
                        link(v.memset(qblk1[:, :, :, :], 0.0))
                    for blk in range(2):
                        wait_drained(dve, ("q", g, blk, 1))
                    for h in range(GH):
                        r = slice(HD * (h % 2), HD * (h % 2) + HD)
                        ins = v.tensor_copy(qblk1[r, :, h // 2, h * NEW:(h + 1) * NEW],
                                            qT1[r, g % 2, h // 2, tok(S_TILE)].rearrange("p (b q) -> p b q", b=STREAMS))
                    ins.then_inc(blocks_done, 1)
                elif kind == "g":
                    _, g, t = job
                    e = gtmp[:, (gate_no[job] - 1) % 2, :]
                    dve.wait_ge(gate_e, gate_no[job])
                    link(v.tensor_scalar(e, e, 1.0, None, ALU.add))
                    link(v.reciprocal(e, e))
                    dst = g1[:, g % 2, t, :] if t < PT_TILES else e
                    v.tensor_tensor(dst, ps(job)[:, 0:GW], e, ALU.mult).then_inc(done, 1)
                elif kind == "gsT":
                    wait_filled(dve, job)
                    v.tensor_copy(gsT[:, job[1] % 2, :, :].rearrange("p a b -> p (a b)"), ps(job)[:, 0:GW]).then_inc(done, 1)
                elif kind == "oT":
                    _, g, t = job
                    wait_filled(dve, job)
                    v.tensor_copy(oT[:, 2 * g:2 * g + 2, tok(t)], ps(job)[:, 0:2 * P].rearrange("p (k n) -> p k n", k=2)).then_inc(done, 1)


_INS = ['x_prompt', 'x_sample', 'cache_mla_ckv', 'cache_mla_krope', 'cache_diff_k', 'cache_diff_v', 'cache_sb_k',
        'cache_sb_v', 'w_in_even', 'q_norm_g', 'w_uq', 'kv_norm_g', 'w_uk', 'w_uv', 'diff_lambda_q',
        'diff_lambda_k', 'diff_subln_g', 'w_out_even', 'ln_even_g', 'ln_even_b', 'w_in_odd', 'w_out_odd',
        'ln_odd_g', 'ln_odd_b']
_OUTS = [(1, SEQ, D), (STREAMS, NEW, D), (1, 1, SEQ, KVL), (1, 1, SEQ, ROT), (1, 1, SEQ, DH, 2, HD),
         (1, 1, SEQ, DH, 2 * HD), (1, 1, SEQ, 16, HD), (1, 1, SEQ, 16, HD), (1, STREAMS, NEW, KVL),
         (1, STREAMS, NEW, ROT), (1, STREAMS, NEW, DH, 2, HD), (1, STREAMS, NEW, DH, 2 * HD),
         (1, STREAMS, NEW, 16, HD), (1, STREAMS, NEW, 16, HD)]


def shape_constants():
    r = np.arange(P)
    neg = np.float32(-1e30)
    masks = np.zeros((P, MASKS), np.float32)
    masks[:, 0:P] = np.where(r[None, :] // 64 <= r[:, None] // 64, 0, neg)
    masks[:, P:2 * P] = np.where(r[None, :] < r[:, None], 0, neg)
    masks[:, 2 * P:] = np.where(r[None, :NEW] < r[:, None] % NEW, 0, neg)
    sel = (r[:, None] // (2 * NEW) * NEW + r[:, None] % NEW == np.arange(DIFF_ROWS)[None, :]).astype(np.float32)
    second = r // NEW % 2
    sign = np.stack([1 - second, second], 1).astype(np.float32)
    pos = np.concatenate([np.arange(SEQ), PAST + r % NEW]).astype(np.float32)

    def rope(rot, theta):
        half = rot // 2
        inv = np.exp(np.float32(-math.log(theta)) * np.arange(half, dtype=np.float32) * np.float32(2.0 / rot))
        ang = pos[:, None] * inv[None, :].astype(np.float32)
        both = np.concatenate([np.cos(ang), np.sin(ang)], 1).astype(np.float32)
        return np.ascontiguousarray(both.reshape(TILES, P, rot).transpose(1, 0, 2))

    return {"c_ident": np.eye(P, dtype=np.float32), "c_masks": masks, "c_sel": sel, "c_sign": sign,
            "c_ropem": rope(ROT, 10000.0), "c_roped": rope(DROT, 500000.0)}


def kernel(**inputs):
    import concourse.bacc as _bacc
    from concourse.bass_utils import run_bass_kernel_spmd as _run

    nc = _bacc.Bacc("TRN2", target_bir_lowering=False, num_devices=1)
    arrays, aps = {}, {}
    for name, x in list((n, inputs[n]) for n in _INS) + list(shape_constants().items()):
        x = np.ascontiguousarray(x)
        arrays[f"in_{name}_dram"] = x
        aps[name] = nc.dram_tensor(f"in_{name}_dram", x.shape, mybir.dt.from_np(x.dtype), kind="ExternalInput").ap()
    outs = [nc.dram_tensor(f"out_{i}_dram", shape, F32, kind="ExternalOutput").ap() for i, shape in enumerate(_OUTS)]
    trunk_kernel(nc, aps, outs)
    r = _run(nc, [arrays], core_ids=[0])
    return tuple(r.results[0][f"out_{i}_dram"] for i in range(len(_OUTS)))
```
